# Optimizing a Trainium2 kernel written in Bass

```python
import jax, jax.numpy as jnp
from jax import lax
import numpy as np

D_MODEL = 1024
BATCH = 1
SEQ = 256
DEPTH = 2

CONV_DIM = D_MODEL // 2
CONV_WIDTH = 31
POOL_WINDOWS = (2, 4, 8, 16)
N_POOL_GROUPS = len(POOL_WINDOWS)
POOL_DIM = D_MODEL // 2
POOL_GROUP_DIM = POOL_DIM // N_POOL_GROUPS
POOL_GROUP_OUT = D_MODEL // N_POOL_GROUPS
IN_SPLITS = (CONV_DIM, 2 * CONV_DIM, 2 * CONV_DIM + POOL_DIM, 2 * CONV_DIM + POOL_DIM + D_MODEL)
IN_COLS = 2 * CONV_DIM + POOL_DIM + 2 * D_MODEL
D_FF = 2816
N_EXPERTS = 8
TOP_K = 2
D_FF_EXPERT = 3584
RMS_EPS = 1e-6
LN_EPS = 1e-5

kernel_name = "hybrid_conv_pool_gated_moe_trunk"

def rms_norm(x, g):
    xf = x.astype(jnp.float32)
    y = xf * lax.rsqrt(jnp.mean(xf * xf, axis=-1, keepdims=True) + RMS_EPS)
    return (y * g.astype(jnp.float32)).astype(x.dtype)

def layer_norm(x, g, b):
    xf = x.astype(jnp.float32)
    mu = jnp.mean(xf, axis=-1, keepdims=True)
    xc = xf - mu
    var = jnp.mean(xc * xc, axis=-1, keepdims=True)
    y = xc * lax.rsqrt(var + LN_EPS) * g.astype(jnp.float32) + b.astype(jnp.float32)
    return y.astype(x.dtype)

def swiglu(h, w_gate, w_up, w_down):
    return (jax.nn.silu(h @ w_gate) * (h @ w_up)) @ w_down

def conformer_conv(a, b, dw, dw_b, ln_g, ln_b, w_conv_out):
    u = a * jax.nn.sigmoid(b)
    u = lax.conv_general_dilated(
        u, dw[:, None, :].astype(u.dtype), window_strides=(1,),
        padding=[(CONV_WIDTH - 1, 0)],
        dimension_numbers=("NWC", "WIO", "NWC"),
        feature_group_count=u.shape[-1]) + dw_b
    u = jax.nn.silu(layer_norm(u, ln_g, ln_b))
    return u @ w_conv_out

def multiscale_pool(p, w_pool, pool_scale):
    B, S, _ = p.shape
    pf = p.astype(jnp.float32).reshape(B, S, N_POOL_GROUPS, POOL_GROUP_DIM)
    cs = jnp.cumsum(pf, axis=1)
    pos = jnp.arange(S, dtype=jnp.int32)
    deltas = []
    for g, w in enumerate(POOL_WINDOWS):
        csg = cs[:, :, g]
        prev = jnp.pad(csg, ((0, 0), (w, 0), (0, 0)))[:, :S]
        count = jnp.minimum(pos + 1, w).astype(jnp.float32)[:, None]
        deltas.append((csg - prev) / count - pf[:, :, g])
    d = jnp.stack(deltas, axis=2).astype(p.dtype)
    y = jnp.einsum("bsgc,gco->bsgo", d, w_pool).reshape(B, S, D_MODEL)
    return y * pool_scale

def hybrid_mixer(h, w_in, conv_dw, conv_dw_b, conv_ln_g, conv_ln_b, w_conv_out,
                 w_pool, pool_scale, w_out):
    proj = h @ w_in
    a, b, p, gc, gp = jnp.split(proj, IN_SPLITS, axis=-1)
    yc = conformer_conv(a, b, conv_dw, conv_dw_b, conv_ln_g, conv_ln_b, w_conv_out)
    yp = multiscale_pool(p, w_pool, pool_scale)
    merged = jax.nn.sigmoid(gc) * yc + jax.nn.sigmoid(gp) * yp
    return merged @ w_out

def moe_ffn(h, router_w, w_gate, w_up, w_down):
    B, S, D = h.shape
    t = h.reshape(B * S, D)
    logits = (t @ router_w).astype(jnp.float32)
    top_v, top_i = lax.top_k(logits, TOP_K)
    top_p = jax.nn.softmax(top_v, axis=-1)
    comb = jnp.sum(jax.nn.one_hot(top_i, N_EXPERTS, dtype=jnp.float32) * top_p[..., None],
                   axis=1).astype(h.dtype)
    y = jnp.zeros_like(t)
    for e in range(N_EXPERTS):
        y = y + comb[:, e:e + 1] * swiglu(t, w_gate[e], w_up[e], w_down[e])
    return y.reshape(B, S, D)

def setup_inputs(seed: int = 0) -> dict:
    key = jax.random.key(seed)
    ks = iter(jax.random.split(key, 32))
    n_dense = (DEPTH + 1) // 2
    n_moe = DEPTH // 2
    f32 = jnp.float32

    def nrm(shape, scale):
        return jax.random.normal(next(ks), shape, f32) * scale

    def gain(shape):
        return 1.0 + 0.02 * jax.random.normal(next(ks), shape, f32)

    return {
        "x": nrm((BATCH, SEQ, D_MODEL), 1.0),
        "mix_norm": gain((DEPTH, D_MODEL)),
        "w_in": nrm((DEPTH, D_MODEL, IN_COLS), D_MODEL ** -0.5),
        "conv_dw": nrm((DEPTH, CONV_WIDTH, CONV_DIM), CONV_WIDTH ** -0.5),
        "conv_dw_b": nrm((DEPTH, CONV_DIM), 0.02),
        "conv_ln_g": gain((DEPTH, CONV_DIM)),
        "conv_ln_b": nrm((DEPTH, CONV_DIM), 0.02),
        "w_conv_out": nrm((DEPTH, CONV_DIM, D_MODEL), CONV_DIM ** -0.5),
        "w_pool": nrm((DEPTH, N_POOL_GROUPS, POOL_GROUP_DIM, POOL_GROUP_OUT), POOL_GROUP_DIM ** -0.5),
        "pool_scale": gain((DEPTH, D_MODEL)),
        "w_out": nrm((DEPTH, D_MODEL, D_MODEL), D_MODEL ** -0.5),
        "ffn_norm": gain((DEPTH, D_MODEL)),
        "dense_w_gate": nrm((n_dense, D_MODEL, D_FF), D_MODEL ** -0.5),
        "dense_w_up": nrm((n_dense, D_MODEL, D_FF), D_MODEL ** -0.5),
        "dense_w_down": nrm((n_dense, D_FF, D_MODEL), D_FF ** -0.5),
        "router_w": nrm((n_moe, D_MODEL, N_EXPERTS), D_MODEL ** -0.5),
        "moe_w_gate": nrm((n_moe, N_EXPERTS, D_MODEL, D_FF_EXPERT), D_MODEL ** -0.5),
        "moe_w_up": nrm((n_moe, N_EXPERTS, D_MODEL, D_FF_EXPERT), D_MODEL ** -0.5),
        "moe_w_down": nrm((n_moe, N_EXPERTS, D_FF_EXPERT, D_MODEL), D_FF_EXPERT ** -0.5),
        "final_norm": gain((D_MODEL,)),
    }

def reference(x, mix_norm, w_in, conv_dw, conv_dw_b, conv_ln_g, conv_ln_b, w_conv_out,
              w_pool, pool_scale, w_out, ffn_norm, dense_w_gate, dense_w_up, dense_w_down,
              router_w, moe_w_gate, moe_w_up, moe_w_down, final_norm):
    for layer in range(DEPTH):
        h = rms_norm(x, mix_norm[layer])
        x = x + hybrid_mixer(h, w_in[layer], conv_dw[layer], conv_dw_b[layer],
                             conv_ln_g[layer], conv_ln_b[layer], w_conv_out[layer],
                             w_pool[layer], pool_scale[layer], w_out[layer])
        h = rms_norm(x, ffn_norm[layer])
        i = layer // 2
        if layer % 2 == 0:
            x = x + swiglu(h, dense_w_gate[i], dense_w_up[i], dense_w_down[i])
        else:
            x = x + moe_ffn(h, router_w[i], moe_w_gate[i], moe_w_up[i], moe_w_down[i])
    return rms_norm(x, final_norm)


_drawn_inputs = setup_inputs


def setup_inputs(seed=0):
    import zlib

    import numpy as np

    out = dict(_drawn_inputs(seed))
    spreads = {}
    factors = {}
    for name, (base, spread) in spreads.items():
        noise = np.random.default_rng([zlib.crc32(name.encode()), seed]).standard_normal(out[name].shape)
        drawn = base * np.exp(spread * noise) if base else spread * noise
        out[name] = __import__('jax').numpy.asarray(drawn.astype(out[name].dtype))
    for name, factor in factors.items():
        out[name] = (out[name] * factor).astype(out[name].dtype)
    return out
```

```python
from contextlib import ExitStack

import concourse.bass as bass
from concourse import mybir

ALU = mybir.AluOpType
ACT = mybir.ActivationFunctionType
AX_X = mybir.AxisListType.X
F32 = mybir.dt.float32
F32R = mybir.dt.float32r
I32 = mybir.dt.int32

P = 128
UNIT = 2048
RAW = 7
RMS_EPS, LN_EPS = 1e-6, 1e-5
SPLIT = 3
OVER = 3
TABLE = 1 + 8 + OVER + 1
NOWHERE = -1000.0


class Seen:

    def __init__(self, per_item):
        self.per_item, self.n, self.item = per_item, {}, None

    def at(self, sem, n):
        per = self.per_item.get(sem.name, 0)
        return n if self.item is None or not per else self.item * per + n

    def next(self, sem, step=1):
        self.n[sem.name] = self.n.get(sem.name, 0) + step
        return self.at(sem, self.n[sem.name])


def trunk_kernel(nc, x, mix_norm, w_in, conv_dw, conv_dw_b, conv_ln_g, conv_ln_b, w_conv_out, w_pool, pool_scale,
                 w_out, ffn_norm, dense_w_gate, dense_w_up, dense_w_down, router_w, moe_w_gate, moe_w_up,
                 moe_w_down, final_norm, out):
    _, S, D = x.shape
    L = w_in.shape[0]
    TAPS, CD = conv_dw.shape[1:]
    GROUPS, GD, GO = w_pool.shape[1:]
    FD = dense_w_gate.shape[2]
    E, _, FE = moe_w_gate.shape[1:]
    TB = S // P
    KD = D // P
    CC = CD // P
    N = 512
    PAD = TAPS - 1
    WINDOWS = (2, 4, 8, 16)
    WPAD = max(WINDOWS)
    FC = FE // N
    DC = FD // N
    assert (TB, KD, CC, GROUPS, FC, DC, FD - DC * N) == (2, 8, 4, 4, 7, 5, 256) and L == 2

    k_rows = lambda w: w.rearrange("(k p) n -> p k n", p=P)

    def slab_units(w, c):
        return [(4, N, lambda j=j: k_rows(w)[:, 4 * j:4 * j + 4, c:c + N]) for j in range(2)]

    def row_units(w, r0, blocks):
        return [(2, D, lambda j=j: k_rows(w)[:, r0 + j:r0 + j + 2, :]) for j in range(0, blocks, 2)]

    def mixer_units(l):
        columns = (CD, 0, 2 * CD) + tuple(3 * CD + N * j for j in range(4))
        units = [u for c in columns for u in slab_units(w_in[l], c)]
        units.append((GROUPS, GO, lambda: w_pool[l].rearrange("g c o -> c g o")))
        return units + row_units(w_conv_out[l], 0, CC) + row_units(w_out[l], 0, KD)

    def dense_units():
        g, u, d = dense_w_gate[0], dense_w_up[0], dense_w_down[0]
        units = []
        for c in range(DC):
            units += slab_units(g, c * N) + slab_units(u, c * N)
            if c:
                units += row_units(d, (c - 1) * 4, 4)
        half = [(4, N, (lambda j=j: k_rows(g)[:, 4 * j:4 * j + 4, DC * N:FD],
                        lambda j=j: k_rows(u)[:, 4 * j:4 * j + 4, DC * N:FD])) for j in range(2)]
        return units + half + row_units(d, (DC - 1) * 4, 4) + row_units(d, DC * 4, 2)

    MIXER = 2 * 7 + 1 + 2 + 4
    STREAM = mixer_units(0) + dense_units() + mixer_units(1)
    U0 = len(STREAM)
    UI = FC * 6
    assert U0 == 2 * MIXER + 33 and U0 % SPLIT == 0 and UI % SPLIT == 0 and UI % RAW == 0

    def item_units(e):
        one = lambda w: w[0, bass.ds(e, 1)].rearrange("a r n -> (a r) n")
        g, u, d = one(moe_w_gate), one(moe_w_up), one(moe_w_down)
        units = []
        for c in range(FC):
            units += slab_units(g, c * N) + slab_units(u, c * N)
            if c:
                units += row_units(d, (c - 1) * 4, 4)
        return units + row_units(d, (FC - 1) * 4, 4)

    unit_width = lambda n: UNIT if n >= U0 else STREAM[n][0] * STREAM[n][1]

    PER_ITEM = dict(hi_ready=UI, lo_ready=UI, unit_used=UI, silu_ready=FC, act_ready=FC,
                    actT_landed=FC, actT_hi=FC, actT_ready=FC, y_ready=1, onehot_ready=1,
                    spread_ready=1, spreadT_landed=1, spreadT_ready=1, scatter_done=4, scatter_added=4, gather_done=2,
                    tokT_hi_ready=KD, tokT_ready=KD)
    landed_at, so_far = [], [0] * RAW
    for n in range(U0 + UI):
        so_far[n % RAW] += 32 if n < U0 and isinstance(STREAM[n][2], tuple) else 16
        landed_at.append(so_far[n % RAW])
    for slot in range(RAW):
        PER_ITEM[f"raw_landed{slot}"] = 16 * UI // RAW

    with ExitStack() as ctx:
        def sb(name, shape, dt=F32):
            return ctx.enter_context(nc.sbuf_tensor(name, shape, dt))

        def sem(name):
            return ctx.enter_context(nc.semaphore(name))

        raw = sb("raw", [P, RAW, UNIT])
        w_hi = sb("w_hi", [P, SPLIT, UNIT], F32R)
        w_lo = sb("w_lo", [P, SPLIT, UNIT], F32R)
        xs = sb("xs", [P, TB, D])
        xn = sb("xn", [P, TB, D])
        hT_hi = sb("hT_hi", [P, KD, S], F32R)
        hT_lo = sb("hT_lo", [P, KD, S], F32R)
        tokA = sb("tokA", [P, TB, N])
        tokP = sb("tokP", [P, TB, N])
        uT = sb("uT", [P, CC, PAD + S])
        pT = sb("pT", [P, GROUPS, WPAD + S])
        win_a = sb("win_a", [P, GROUPS, WPAD + S])
        win_b = sb("win_b", [P, GROUPS, WPAD + S])
        inv_count = sb("inv_count", [P, GROUPS, S])
        conv = xn[:, 0, :].rearrange("p (c t) -> p c t", c=CC)
        gate_c = sb("gate_c", [P, TB, D])
        gate_p = sb("gate_p", [P, TB, D])
        cT_hi = sb("cT_hi", [P, CC * S], F32R)
        cT_lo = sb("cT_lo", [P, CC * S], F32R)
        dT_hi = sb("dT_hi", [P, GROUPS * S], F32R)
        dT_lo = sb("dT_lo", [P, GROUPS * S], F32R)
        row_gain = sb("row_gain", [P, D])
        ident = sb("ident", [P, P])
        ones = sb("ones", [P, P])
        mean_w = sb("mean_w", [P, P])
        before = sb("before", [P, P])
        slot_no = sb("slot_no", [P, P])
        vecs = sb("vecs", [P, 56])
        taps = sb("taps", [P, 2, 124])
        small = sb("small", [P, 16])
        rw = sb("rw", [P, KD, E])
        route = sb("route", [P, 16, TB, E])
        rev = sb("rev", [P, TB, E])
        over = sb("over", [P, 8, E])
        pair = sb("pair", [P, 12, TB])
        slot_of = sb("slot_of", [P, TABLE * TB])
        comb_of = sb("comb_of", [P, TABLE * TB])
        items = sb("items", [P, 8], I32)
        onehot, spread, spreadT = (uT[:, c, 0:TB * P].rearrange("p (b t) -> p b t", b=TB) for c in range(3))
        vec_rows = xn[:, 0, 0:P]
        tap_rows = xn[:, 0, P:3 * P].rearrange("p (l c) -> p l c", l=L)
        slot_int = win_b[:, 0, WPAD:WPAD + P].bitcast(I32)
        sq, junk, y = xn[:, 1, :], gate_c[:, 0, :], gate_p[:, 0, :]
        ln_std, ln_rstd = sq[:, 0:S], sq[:, S:2 * S]
        act_hi = cT_hi[:, :].rearrange("p (b f t) -> p b f t", b=TB, f=4)
        act_lo = cT_lo[:, :].rearrange("p (b f t) -> p b f t", b=TB, f=4)
        tokT_hi = dT_hi[:, :].rearrange("p (k t) -> p k t", k=KD)
        tokT_lo = dT_lo[:, :].rearrange("p (k t) -> p k t", k=KD)
        bank = [ctx.enter_context(nc.psum_tensor(f"bank{i}", [P, N], F32)) for i in range(8)]

        raw_landed = [sem(f"raw_landed{i}") for i in range(RAW)]
        hi_ready, lo_ready, unit_used = sem("hi_ready"), sem("lo_ready"), sem("unit_used")
        x_landed, vecs_landed, rw_landed = sem("x_landed"), sem("vecs_landed"), sem("rw_landed")
        gain_landed, consts_ready, pool_step = sem("gain_landed"), sem("consts_ready"), sem("pool_step")
        vecT_done, vecs_ready = sem("vecT_done"), sem("vecs_ready")
        result_ready, out_stored = sem("result_ready"), sem("out_stored")
        sumsq_ready, meansq_ready, rstd_ready = sem("sumsq_ready"), sem("meansq_ready"), sem("rstd_ready")
        xn_ready, xT_done, hT_hi_ready, hT_ready = sem("xn_ready"), sem("xT_done"), sem("hT_hi_ready"), sem("hT_ready")
        x_ready, dve_step = sem("x_ready"), sem("dve_step")
        sig_ready, u_ready, p_ready = sem("sig_ready"), sem("u_ready"), sem("p_ready")
        gates_ready, gate_p_scaled = sem("gates_ready"), sem("gate_p_scaled")
        uT_done, uT_ready, pT_done, pT_ready = sem("uT_done"), sem("uT_ready"), sem("pT_done"), sem("pT_ready")
        conv_step, conv_ready = sem("conv_step"), sem("conv_ready")
        pooled_ready, dT_hi_ready, dT_ready = sem("pooled_ready"), sem("dT_hi_ready"), sem("dT_ready")
        mean_done, centred, centred_sq, var_done = sem("mean_done"), sem("centred"), sem("centred_sq"), sem("var_done")
        std_ready, normed, silu_conv = sem("std_ready"), sem("normed"), sem("silu_conv")
        cT_hi_ready, cT_ready = sem("cT_hi_ready"), sem("cT_ready")
        yp_merged, merged_ready = sem("yp_merged"), sem("merged_ready")
        silu_ready, act_ready = sem("silu_ready"), sem("act_ready")
        actT_landed, actT_hi, actT_ready = sem("actT_landed"), sem("actT_hi"), sem("actT_ready")
        y_ready = sem("y_ready")
        logits_done, diff_ready, probs_ready = sem("logits_done"), sem("diff_ready"), sem("probs_ready")
        mask_ready, rank_done, tables_ready = sem("mask_ready"), sem("rank_done"), sem("tables_ready")
        onehot_ready, gather_done = sem("onehot_ready"), sem("gather_done")
        tokT_hi_ready, tokT_ready = sem("tokT_hi_ready"), sem("tokT_ready")
        spread_ready, spreadT_landed, spreadT_ready = sem("spread_ready"), sem("spreadT_landed"), sem("spreadT_ready")
        scatter_done, scatter_added = sem("scatter_done"), sem("scatter_added")

        V_MIX, V_FFN, V_CB, V_LG, V_LB = 0, 16, 32, 40, 48

        block = ctx.enter_context(nc.Block())


        @block.sync
        def _(sp):
            seen = Seen(PER_ITEM)

            def load(n, unit):
                blocks, width, source = unit
                if n >= RAW:
                    sp.wait_ge(lo_ready, seen.at(lo_ready, n - RAW + 1))
                dst = raw[:, n % RAW, 0:blocks * width].rearrange("p (k n) -> p k n", k=blocks)
                if isinstance(source, tuple):
                    half = width // 2
                    sp.dma_start(dst[:, :, 0:half], source[0]()).then_inc(raw_landed[n % RAW], 16)
                    sp.dma_start(dst[:, :, half:], source[1]()).then_inc(raw_landed[n % RAW], 16)
                else:
                    sp.dma_start(dst, source()).then_inc(raw_landed[n % RAW], 16)

            sp.dma_start(xs[:, :, :], x[0].rearrange("(b p) d -> p b d", p=P)).then_inc(x_landed, 16)
            for n, unit in enumerate(STREAM):
                load(n, unit)
            with sp.Fori(0, E) as i:
                seen.item = i
                for j, unit in enumerate(item_units(i)):
                    load(U0 + j, unit)
            seen.item = None
            sp.wait_ge(tables_ready, 2)
            n_items = sp.value_load(items[0:1, 0:1], min_val=E, max_val=E + OVER)
            with sp.If(n_items > E):
                with sp.Fori(E, n_items) as i:
                    seen.item = i
                    e = sp.value_load(items[0:1, bass.ds(i - (E - 1), 1)], min_val=0, max_val=E - 1)
                    for j, unit in enumerate(item_units(e)):
                        load(U0 + j, unit)
            for b in range(TB):
                sp.wait_ge(result_ready, b + 1)
                sp.dma_start(out[0, b * P:(b + 1) * P, :], xs[:, b, :]).then_inc(out_stored, 16)
            sp.wait_ge(out_stored, 16 * TB)

        @block.gpsimd
        def _(pool):
            seen = Seen(PER_ITEM)
            steps = [0]

            def step(ins):
                steps[0] += 1
                ins.then_inc(pool_step, 1)
                pool.wait_ge(pool_step, steps[0])

            rows = 0
            for v, per in ((mix_norm, KD), (ffn_norm, KD), (conv_dw_b, CC), (conv_ln_g, CC), (conv_ln_b, CC)):
                pool.dma_start(vec_rows[rows:rows + L * per, :], v.rearrange("l (k p) -> (l k) p", p=P)).then_inc(vecs_landed, 16)
                rows += L * per
            for l in range(L):
                pool.dma_start(tap_rows[0:TAPS * CC, l, :], conv_dw[l].rearrange("j (c p) -> (j c) p", p=P)).then_inc(vecs_landed, 16)
            pool.dma_start(row_gain[:, :], pool_scale[0:1, :].to_broadcast([P, D])).then_inc(gain_landed, 16)
            pool.dma_start(rw[:, :, :], router_w[0].rearrange("(k p) e -> p k e", p=P)).then_inc(rw_landed, 16)

            step(pool.memset(ident[:, :], 0.0))
            step(pool.affine_select(out=ident[:, :], in_=ident[:, :], compare_op=ALU.not_equal, fill=1.0, base=0,
                                    pattern=[[-1, P]], channel_multiplier=1))
            pool.memset(small[:, 4:6], -0.5)
            pool.memset(small[:, 13:14], LN_EPS)
            pool.memset(uT[:, :, 0:PAD], 0.0)
            pool.memset(pT[:, :, 0:WPAD], 0.0)
            pool.memset(win_a[:, :, 0:WPAD], 0.0)
            pool.memset(win_b[:, :, 0:WPAD], 0.0)
            step(pool.memset(mean_w[:, :], 1.0 / CD))
            pool.memset(small[:, 12:13], 0.0).then_inc(consts_ready, 1)
            step(pool.memset(ones[:, :], 1.0))
            step(pool.affine_select(out=before[:, :], in_=ones[:, :], compare_op=ALU.is_gt, fill=0.0, base=0,
                                    pattern=[[1, P]], channel_multiplier=-1))
            step(pool.iota(slot_int[:, :], pattern=[[1, P]], base=0, channel_multiplier=0))
            step(pool.tensor_copy(slot_no[:, :], slot_int[:, :]))
            for e in range(E):
                pool.memset(rev[:, :, e:e + 1], float(E - e))
            pool.memset(slot_of[:, :], NOWHERE)
            pool.memset(comb_of[:, :], 0.0)
            for g, w in enumerate(WINDOWS):
                pool.memset(inv_count[:, g, w - 1:S], 1.0 / w)
                for t in range(w - 1):
                    last = pool.memset(inv_count[:, g, t:t + 1], 1.0 / (t + 1))
            step(last)
            pool.memset(small[:, 12:13], 0.0).then_inc(consts_ready, 1)

            def inverse_root():
                pool.wait_ge(meansq_ready, seen.next(meansq_ready))
                pool.tensor_tensor(small[:, 6:8], small[:, 2:4], small[:, 4:6], ALU.pow).then_inc(rstd_ready, 1)

            for l in range(L):
                inverse_root()
                pool.wait_ge(pT_ready, seen.next(pT_ready, 2))
                src = pT
                for i, (dst, sh) in enumerate(((win_a, 1), (win_b, 2), (win_a, 4), (win_b, 8))):
                    step(pool.tensor_tensor(dst[:, i:, WPAD:], src[:, i:, WPAD:], src[:, i:, WPAD - sh:WPAD + S - sh], ALU.add))
                    step(pool.tensor_tensor(dst[:, i, WPAD:], dst[:, i, WPAD:], inv_count[:, i, :], ALU.mult))
                    pool.tensor_tensor(dst[:, i, WPAD:], dst[:, i, WPAD:], pT[:, i, WPAD:], ALU.subtract).then_inc(pooled_ready, 1)
                    src = dst
                pool.wait_ge(gain_landed, seen.next(gain_landed, 16))
                pool.wait_ge(gates_ready, seen.next(gates_ready, 4 * TB))
                for b in range(TB):
                    pool.tensor_tensor(gate_p[:, b, :], gate_p[:, b, :], row_gain[:, :], ALU.mult).then_inc(gate_p_scaled, 1)
                pool.wait_ge(gate_p_scaled, TB * (l + 1))
                row = pool_scale[l + 1:l + 2, :] if l + 1 < L else final_norm.rearrange("(a d) -> a d", a=1)
                pool.dma_start(row_gain[:, :], row.to_broadcast([P, D])).then_inc(gain_landed, 16)
                inverse_root()
            inverse_root()

        def run_items(eng, seen, unit, item):
            base = dict(seen.n)
            with eng.Fori(0, E) as i:
                seen.item, unit[0] = i, U0
                item(i)
            seen.item = None
            eng.wait_ge(tables_ready, 2)
            n_items = eng.value_load(items[0:1, 0:1], min_val=E, max_val=E + OVER)
            for name, n in seen.n.items():
                assert n - base.get(name, 0) == (PER_ITEM[name] if n != base.get(name, 0) else 0), name
            with eng.If(n_items > E):
                with eng.Fori(E, n_items) as i:
                    seen.n = dict(base)
                    seen.item, unit[0] = i, U0
                    item(i)
            seen.n, seen.item = dict(base), n_items
            return n_items

        @block.scalar
        def _(act):
            seen = Seen(PER_ITEM)
            unit = [0]

            def split_to(n):
                while unit[0] < n:
                    u = unit[0]
                    act.wait_ge(raw_landed[u % RAW], seen.at(raw_landed[u % RAW], landed_at[u]))
                    if u >= SPLIT:
                        act.wait_ge(unit_used, seen.at(unit_used, u - SPLIT + 1))
                    width = unit_width(u)
                    act.activation(w_hi[:, u % SPLIT, 0:width], raw[:, u % RAW, 0:width], ACT.Copy).then_inc(hi_ready, 1)
                    unit[0] += 1

            def sums_of_squares():
                for b in range(TB):
                    act.activation(junk, xs[:, b, :], ACT.Square, accum_out=small[:, b:b + 1]).then_inc(sumsq_ready, 1)
                    act.wait_ge(sumsq_ready, seen.next(sumsq_ready))

            def operand(gain):
                for k in range(KD):
                    if k % 2 == 0:
                        act.wait_ge(xT_done, seen.next(xT_done))
                    scale = 1.0 if gain is None else vecs[:, gain + k:gain + k + 1]
                    act.activation(hT_hi[:, k, :], bank[4 + k // 2][:, (k % 2) * S:(k % 2 + 1) * S], ACT.Copy,
                                   scale=scale).then_inc(hT_hi_ready, 1)

            def mixer(l, U):
                split_to(U + 3)
                operand(V_MIX + KD * l)
                split_to(U + 5)
                act.wait_ge(unit_used, seen.at(unit_used, U + 2))
                for b in range(TB):
                    act.activation(tokA[:, b, :], bank[b][:, :], ACT.Sigmoid).then_inc(sig_ready, 1)
                split_to(U + 9)
                act.wait_ge(unit_used, seen.at(unit_used, U + 6))
                for b in range(TB):
                    act.activation(tokP[:, b, :], bank[b][:, :], ACT.Copy).then_inc(p_ready, 1)
                for j in range(2):
                    act.wait_ge(uT_done, seen.next(uT_done))
                    act.activation(uT[:, 2 * j:2 * j + 2, PAD:], bank[4 + j][:, :].rearrange("p (c t) -> p c t", c=2),
                                   ACT.Copy).then_inc(uT_ready, 1)
                for s in range(4):
                    split_to(U + 11 + 2 * s)
                    dst, c = (gate_c, gate_p)[s // 2], (s % 2) * N
                    act.wait_ge(unit_used, seen.at(unit_used, U + 8 + 2 * s))
                    for b in range(TB):
                        act.activation(dst[:, b, c:c + N], bank[2 * ((s + 1) % 2) + b][:, :], ACT.Sigmoid).then_inc(gates_ready, 1)
                    if s == 0:
                        for j in range(2):
                            act.wait_ge(pT_done, seen.next(pT_done))
                            act.activation(pT[:, 2 * j:2 * j + 2, WPAD:], bank[6 + j][:, :].rearrange("p (c t) -> p c t", c=2),
                                           ACT.Copy).then_inc(pT_ready, 1)
                for g in range(GROUPS):
                    act.wait_ge(pooled_ready, seen.next(pooled_ready))
                    act.activation(dT_hi[:, g * S:(g + 1) * S], (win_a, win_b)[g % 2][:, g, WPAD:], ACT.Copy).then_inc(dT_hi_ready, 1)
                act.wait_ge(centred, seen.next(centred))
                act.activation(sq, xn[:, 0, :], ACT.Square).then_inc(centred_sq, 1)
                act.wait_ge(var_done, seen.next(var_done))
                act.activation(ln_std[:, :], bank[5][:, 0:S], ACT.Sqrt, bias=small[:, 13:14]).then_inc(std_ready, 1)
                split_to(U + 18)
                act.wait_ge(normed, seen.next(normed))
                for c in range(CC):
                    g, b = V_LG + CC * l + c, V_LB + CC * l + c
                    act.activation(conv[:, c, :], conv[:, c, :], ACT.Silu, bias=vecs[:, b:b + 1], scale=vecs[:, g:g + 1]).then_inc(silu_conv, 1)
                for c in range(CC):
                    act.wait_ge(silu_conv, seen.next(silu_conv))
                    act.activation(cT_hi[:, c * S:(c + 1) * S], conv[:, c, :], ACT.Copy).then_inc(cT_hi_ready, 1)
                split_to(U + 20)
                operand(None)
                split_to(U + 21)

            def silu_of_gate(c, g, width):
                act.wait_ge(unit_used, seen.at(unit_used, g + 2))
                for b in range(TB):
                    if c:
                        act.wait_ge(act_ready, seen.at(act_ready, TB * (c - 1) + b + 1))
                    act.activation(tokA[:, b, 0:width], bank[b][:, 0:width], ACT.Silu).then_inc(silu_ready, 1)

            def hidden_hi(n):
                for b in range(TB):
                    act.wait_ge(actT_landed, seen.next(actT_landed))
                    act.activation(act_hi[:, b, 0:n, :], bank[2 + b][:, 0:n * P].rearrange("p (f t) -> p f t", f=n),
                                   ACT.Copy).then_inc(actT_hi, 1)

            act.wait_ge(x_landed, 16)
            sums_of_squares()
            for i, (dst, n) in enumerate(((vecs[:, :], 56), (taps[:, 0, :], 124), (taps[:, 1, :], 124))):
                act.wait_ge(vecT_done, seen.next(vecT_done))
                act.activation(dst, bank[i][:, 0:n], ACT.Copy).then_inc(vecs_ready, 1)
            act.wait_ge(vecs_ready, 3)
            act.wait_ge(consts_ready, 1)
            mixer(0, 0)

            U = MIXER
            split_to(U + 2)
            act.wait_ge(x_ready, seen.next(x_ready, TB))
            sums_of_squares()
            split_to(U + 3)
            operand(V_FFN)
            for c in range(DC + 1):
                g = U + max(0, 6 * c - 2)
                split_to(g + 4)
                if c:
                    hidden_hi(4)
                split_to(g + 5)
                silu_of_gate(c, g, N if c < DC else N // 2)
            hidden_hi(2)

            U = MIXER + 33
            split_to(U + 2)
            act.wait_ge(x_ready, seen.next(x_ready, TB))
            sums_of_squares()
            mixer(1, U)

            act.wait_ge(x_ready, seen.next(x_ready, TB))
            sums_of_squares()
            operand(V_FFN + KD)
            act.wait_ge(diff_ready, seen.next(diff_ready))
            act.activation(pair[:, 8, :], pair[:, 7, :], ACT.Sigmoid).then_inc(probs_ready, 1)
            act.activation(pair[:, 9, :], pair[:, 7, :], ACT.Sigmoid, scale=-1.0).then_inc(probs_ready, 1)

            def gathered_hi():
                for k in range(KD):
                    if k % 4 == 0:
                        act.wait_ge(gather_done, seen.next(gather_done))
                    g = V_FFN + KD + k
                    act.activation(tokT_hi[:, k, :], bank[6 + k // 4][:, (k % 4) * P:(k % 4 + 1) * P], ACT.Copy,
                                   scale=vecs[:, g:g + 1]).then_inc(tokT_hi_ready, 1)

            def result_of_item():
                act.wait_ge(unit_used, seen.at(unit_used, U0))
                act.activation(y[:, 0:N], bank[4][:, :], ACT.Copy)
                act.activation(y[:, N:], bank[5][:, :], ACT.Copy).then_inc(y_ready, 1)

            def scatter_matrix():
                act.wait_ge(spreadT_landed, seen.next(spreadT_landed))
                act.activation(spreadT[:, :, :], bank[3][:, 0:TB * P].rearrange("p (b t) -> p b t", b=TB),
                               ACT.Copy).then_inc(spreadT_ready, 1)

            def item_hidden_hi():
                act.wait_ge(actT_landed, seen.next(actT_landed))
                act.activation(act_hi[:, 0, :, :], bank[2][:, :].rearrange("p (f t) -> p f t", f=4), ACT.Copy).then_inc(actT_hi, 1)

            gathered_hi()
            used_before = TB * (DC + 1)

            def item(i):
                split_to(U0 + 3)
                result_of_item()
                for c in range(FC):
                    g = U0 + max(0, 6 * c - 2)
                    split_to(g + 4)
                    if c:
                        item_hidden_hi()
                    if c == 1:
                        scatter_matrix()
                    split_to(g + 5)
                    act.wait_ge(unit_used, seen.at(unit_used, g + 2))
                    act.wait_ge(act_ready, seen.at(act_ready, used_before + c))
                    act.activation(tokA[:, 0, :], bank[0][:, :], ACT.Silu).then_inc(silu_ready, 1)
                split_to(U0 + UI - 2)
                act.wait_ge(unit_used, seen.at(unit_used, U0 + UI - 4))
                gathered_hi()
                split_to(U0 + UI)
                item_hidden_hi()

            run_items(act, seen, unit, item)
            result_of_item()
            scatter_matrix()
            act.wait_ge(scatter_added, seen.at(scatter_added, 2 * TB))
            sums_of_squares()

        @block.vector
        def _(dve):
            seen = Seen(PER_ITEM)
            unit = [0]
            steps = [0]

            def step(ins):
                steps[0] += 1
                ins.then_inc(dve_step, 1)
                dve.wait_ge(dve_step, steps[0])

            def split_to(n):
                while unit[0] < n:
                    u = unit[0]
                    dve.wait_ge(hi_ready, seen.at(hi_ready, u + 1))
                    width = unit_width(u)
                    dve.tensor_tensor(w_lo[:, u % SPLIT, 0:width], raw[:, u % RAW, 0:width],
                                      w_hi[:, u % SPLIT, 0:width].bitcast(F32), ALU.subtract).then_inc(lo_ready, 1)
                    unit[0] += 1

            def normalise(gain=None):
                dve.wait_ge(sumsq_ready, seen.next(sumsq_ready, TB))
                dve.tensor_scalar(small[:, 2:4], small[:, 0:2], 1.0 / D, RMS_EPS, ALU.mult, ALU.add).then_inc(meansq_ready, 1)
                dve.wait_ge(rstd_ready, seen.next(rstd_ready))
                for b in range(TB):
                    rstd = small[:, 6 + b:7 + b]
                    if gain is None:
                        dve.tensor_scalar(xn[:, b, :], xs[:, b, :], rstd, None, ALU.mult).then_inc(xn_ready, 1)
                    else:
                        dve.scalar_tensor_tensor(xs[:, b, :], xs[:, b, :], rstd, gain, ALU.mult, ALU.mult).then_inc(result_ready, 1)

            def operand(gain):
                for k in range(KD):
                    if k % 2 == 0:
                        dve.wait_ge(hT_hi_ready, seen.next(hT_hi_ready, 2))
                    src = bank[4 + k // 2][:, (k % 2) * S:(k % 2 + 1) * S]
                    scale = 1.0 if gain is None else vecs[:, gain + k:gain + k + 1]
                    dve.scalar_tensor_tensor(hT_lo[:, k, :], src, scale, hT_hi[:, k, :].bitcast(F32),
                                             ALU.mult, ALU.subtract).then_inc(hT_ready, 1)

            conv_steps = [0]

            def conv_tap(l, j):
                for c in range(CC):
                    if j:
                        dve.wait_ge(conv_step, conv_steps[0] - CC + 1)
                    tap = taps[:, l, CC * j + c:CC * j + c + 1]
                    src = uT[:, c, j:j + S]
                    if j == 0:
                        bias = vecs[:, V_CB + CC * l + c:V_CB + CC * l + c + 1]
                        ins = dve.tensor_scalar(conv[:, c, :], src, tap, bias, ALU.mult, ALU.add)
                    else:
                        ins = dve.scalar_tensor_tensor(conv[:, c, :], src, tap, conv[:, c, :], ALU.mult, ALU.add)
                    ins.then_inc(conv_step, 1)
                    conv_steps[0] += 1

            def mixer(l, U):
                normalise()
                split_to(U + 3)
                operand(V_MIX + KD * l)
                split_to(U + 7)
                for b in range(TB):
                    dve.wait_ge(sig_ready, seen.next(sig_ready))
                    dve.wait_ge(unit_used, seen.at(unit_used, U + 4))
                    dve.tensor_tensor(tokA[:, b, :], bank[2 + b][:, :], tokA[:, b, :], ALU.mult).then_inc(u_ready, 1)
                split_to(U + 9)
                dve.wait_ge(uT_ready, seen.next(uT_ready, 2))
                for j in range(TAPS):
                    if j and j % 3 == 0:
                        split_to(min(U + 9 + j // 3, U + 17))
                    conv_tap(l, j)
                split_to(U + 17)
                dve.wait_ge(conv_step, conv_steps[0])
                dve.memset(small[:, 11:12], 0.0).then_inc(conv_ready, 1)
                for g in range(GROUPS):
                    dve.wait_ge(dT_hi_ready, seen.next(dT_hi_ready))
                    dve.tensor_tensor(dT_lo[:, g * S:(g + 1) * S], (win_a, win_b)[g % 2][:, g, WPAD:],
                                      dT_hi[:, g * S:(g + 1) * S].bitcast(F32), ALU.subtract).then_inc(dT_ready, 1)
                dve.wait_ge(mean_done, seen.next(mean_done))
                dve.tensor_tensor(conv[:, :, :], conv[:, :, :], bank[4][:, 0:S].unsqueeze(1).to_broadcast([P, CC, S]),
                                  ALU.subtract).then_inc(centred, 1)
                for b in range(TB):
                    dve.wait_ge(unit_used, seen.at(unit_used, U + 15))
                    dve.wait_ge(gate_p_scaled, seen.next(gate_p_scaled))
                    for h in range(2):
                        part = gate_p[:, b, h * N:(h + 1) * N]
                        dve.tensor_tensor(part, bank[2 * b + h][:, :], part, ALU.mult).then_inc(yp_merged, 1)
                dve.wait_ge(std_ready, seen.next(std_ready))
                step(dve.reciprocal(ln_rstd[:, :], ln_std[:, :]))
                dve.tensor_tensor(conv[:, :, :], conv[:, :, :], ln_rstd[:, :].unsqueeze(1).to_broadcast([P, CC, S]),
                                  ALU.mult).then_inc(normed, 1)
                split_to(U + 18)
                for c in range(CC):
                    dve.wait_ge(cT_hi_ready, seen.next(cT_hi_ready))
                    dve.tensor_tensor(cT_lo[:, c * S:(c + 1) * S], conv[:, c, :], cT_hi[:, c * S:(c + 1) * S].bitcast(F32),
                                      ALU.subtract).then_inc(cT_ready, 1)
                split_to(U + 20)
                dve.wait_ge(unit_used, seen.at(unit_used, U + 17))
                for b in range(TB):
                    for h in range(2):
                        part = gate_c[:, b, h * N:(h + 1) * N]
                        step(dve.tensor_tensor(part, bank[2 * b + h][:, :], part, ALU.mult))
                    dve.tensor_tensor(gate_c[:, b, :], gate_c[:, b, :], gate_p[:, b, :], ALU.add).then_inc(merged_ready, 1)
                operand(None)
                split_to(U + 21)
                add_to_x(U + 21, 0)

            def add_to_x(units, first_bank):
                dve.wait_ge(unit_used, seen.at(unit_used, units))
                for b in range(TB):
                    for h in range(2):
                        part = xs[:, b, h * N:(h + 1) * N]
                        ins = dve.tensor_tensor(part, bank[first_bank + 2 * b + h][:, :], part, ALU.add)
                    ins.then_inc(x_ready, 1)

            def hidden_lo(n):
                for b in range(TB):
                    dve.wait_ge(actT_hi, seen.next(actT_hi))
                    dve.tensor_tensor(act_lo[:, b, 0:n, :], bank[2 + b][:, 0:n * P].rearrange("p (f t) -> p f t", f=n),
                                      act_hi[:, b, 0:n, :].bitcast(F32), ALU.subtract).then_inc(actT_ready, 1)

            dve.wait_ge(x_landed, 16)
            dve.wait_ge(vecs_ready, 3)
            mixer(0, 0)

            U = MIXER
            split_to(U + 2)
            normalise()
            split_to(U + 3)
            operand(V_FFN)
            for c in range(DC + 1):
                g = U + max(0, 6 * c - 2)
                split_to(g + 4)
                if c:
                    hidden_lo(4)
                split_to(min(g + 7, U + 33))
                if c < DC:
                    dve.wait_ge(unit_used, seen.at(unit_used, g + 4))
                for b in range(TB):
                    dve.wait_ge(silu_ready, seen.next(silu_ready))
                    if c < DC:
                        up, width = bank[2 + b][:, :], N
                    else:
                        up, width = bank[b][:, N // 2:], N // 2
                    dve.tensor_tensor(tokP[:, b, 0:width], up, tokA[:, b, 0:width], ALU.mult).then_inc(act_ready, 1)
            hidden_lo(2)
            add_to_x(U + 33, 4)

            U = MIXER + 33
            split_to(U + 2)
            mixer(1, U)

            normalise()
            operand(V_FFN + KD)

            per_e = lambda v: v.unsqueeze(2).to_broadcast([P, TB, E])
            LG, EQ, CAND, SEL1, LG2, SEL2, MASK, POS, T1, T2, COMB = range(11)
            r = lambda i: route[:, i, :, :]
            dve.wait_ge(consts_ready, 2)
            dve.wait_ge(logits_done, seen.next(logits_done))
            step(dve.tensor_copy(r(LG), bank[0][:, 0:TB * E].rearrange("p (b e) -> p b e", b=TB)))

            def best(values, v, sel):
                step(dve.tensor_reduce(pair[:, v, :], r(values), AX_X, ALU.max))
                step(dve.tensor_tensor(r(EQ), r(values), per_e(pair[:, v, :]), ALU.is_equal))
                step(dve.tensor_tensor(r(CAND), r(EQ), rev[:, :, :], ALU.mult))
                step(dve.tensor_reduce(pair[:, 2, :], r(CAND), AX_X, ALU.max))
                step(dve.tensor_tensor(r(sel), rev[:, :, :], per_e(pair[:, 2, :]), ALU.is_equal))

            best(LG, 0, SEL1)
            step(dve.scalar_tensor_tensor(r(LG2), r(SEL1), -3.0e38, r(LG), ALU.mult, ALU.add))
            best(LG2, 1, SEL2)
            step(dve.tensor_tensor(pair[:, 7, :], pair[:, 0, :], pair[:, 1, :], ALU.subtract))
            dve.memset(small[:, 11:12], 0.0).then_inc(diff_ready, 1)
            step(dve.tensor_tensor(r(MASK), r(SEL1), r(SEL2), ALU.add))
            dve.memset(small[:, 11:12], 0.0).then_inc(mask_ready, 1)
            dve.wait_ge(probs_ready, seen.next(probs_ready, 2))
            step(dve.tensor_tensor(r(T1), r(SEL1), per_e(pair[:, 8, :]), ALU.mult))
            step(dve.tensor_tensor(r(T2), r(SEL2), per_e(pair[:, 9, :]), ALU.mult))
            dve.wait_ge(rank_done, seen.next(rank_done))
            step(dve.scalar_tensor_tensor(r(POS), bank[3][:, 0:TB * E].rearrange("p (b e) -> p b e", b=TB), -NOWHERE,
                                          r(MASK), ALU.add, ALU.mult))
            table = lambda t, i, n: t[:, i * TB:(i + n) * TB].rearrange("p (i b) -> p b i", b=TB)
            step(dve.tensor_scalar(r(POS), r(POS), NOWHERE, None, ALU.add))
            step(dve.tensor_tensor(r(COMB), r(T1), r(T2), ALU.add))
            step(dve.tensor_copy(table(slot_of, 1, E), r(POS)))
            step(dve.tensor_copy(table(comb_of, 1, E), r(COMB)))
            dve.memset(small[:, 11:12], 0.0).then_inc(tables_ready, 1)

            def gather_matrix(column):
                for b in range(TB):
                    ins = dve.tensor_scalar(onehot[:, b, :], slot_no[:, :], slot_of[:, bass.ds(column * TB + b, 1)], None, ALU.is_equal)
                ins.then_inc(onehot_ready, 1)

            gather_matrix(1)

            OVM, RANK, SELK, PROD, IDX = range(5)
            v = lambda i: over[:, i, :]
            step(dve.tensor_scalar(v(OVM), bank[3][:, TB * E:(TB + 1) * E], float(P), None, ALU.is_gt))
            step(dve.memset(over[:, RANK, 0:1], 0.0))
            for e in range(1, E):
                step(dve.tensor_tensor(over[:, RANK, e:e + 1], over[:, RANK, e - 1:e], over[:, OVM, e - 1:e], ALU.add))
            step(dve.tensor_scalar(v(IDX), rev[:, 0, :], -1.0, float(E), ALU.mult, ALU.add))
            step(dve.tensor_reduce(small[:, 8:9], v(OVM), AX_X, ALU.add))
            step(dve.tensor_scalar(items[:, 0:1], small[:, 8:9], float(E), None, ALU.add))
            for k in range(OVER):
                step(dve.scalar_tensor_tensor(v(SELK), v(RANK), float(k), v(OVM), ALU.is_equal, ALU.mult))
                step(dve.tensor_tensor(v(PROD), v(SELK), v(IDX), ALU.mult))
                step(dve.tensor_reduce(small[:, 8:9], v(PROD), AX_X, ALU.add))
                step(dve.tensor_copy(items[:, 1 + k:2 + k], small[:, 8:9]))
                step(dve.tensor_reduce(small[:, 9:10], v(SELK), AX_X, ALU.add))
                step(dve.tensor_scalar(small[:, 10:11], small[:, 9:10], -NOWHERE - P, NOWHERE, ALU.mult, ALU.add))
                for src, dst, shift in ((POS, slot_of, True), (COMB, comb_of, False)):
                    step(dve.tensor_tensor(r(T1), r(src), v(SELK).unsqueeze(1).to_broadcast([P, TB, E]), ALU.mult))
                    step(dve.tensor_reduce(pair[:, 3, :], r(T1), AX_X, ALU.add))
                    col = dst[:, (1 + E + k) * TB:(2 + E + k) * TB]
                    if shift:
                        step(dve.tensor_scalar(col, pair[:, 3, :], small[:, 10:11], None, ALU.add))
                    else:
                        step(dve.tensor_copy(col, pair[:, 3, :]))
            dve.memset(small[:, 11:12], 0.0).then_inc(tables_ready, 1)

            def gathered_lo():
                for k in range(KD):
                    if k % 4 == 0:
                        dve.wait_ge(tokT_hi_ready, seen.next(tokT_hi_ready, 4))
                    g = V_FFN + KD + k
                    dve.scalar_tensor_tensor(tokT_lo[:, k, :], bank[6 + k // 4][:, (k % 4) * P:(k % 4 + 1) * P],
                                             vecs[:, g:g + 1], tokT_hi[:, k, :].bitcast(F32), ALU.mult,
                                             ALU.subtract).then_inc(tokT_ready, 1)

            def scatter_weights(column):
                for b in range(TB):
                    ins = dve.tensor_scalar(spread[:, b, :], slot_no[:, :], slot_of[:, bass.ds(column * TB + b, 1)],
                                            comb_of[:, bass.ds(column * TB + b, 1)], ALU.is_equal, ALU.mult)
                ins.then_inc(spread_ready, 1)

            def add_scattered(b):
                for h in range(2):
                    dve.wait_ge(scatter_done, seen.next(scatter_done))
                    part = xs[:, b, h * N:(h + 1) * N]
                    dve.tensor_tensor(part, bank[6 + h][:, :], part, ALU.add).then_inc(scatter_added, 1)

            def item_hidden_lo():
                dve.wait_ge(actT_hi, seen.next(actT_hi))
                dve.tensor_tensor(act_lo[:, 0, :, :], bank[2][:, :].rearrange("p (f t) -> p f t", f=4),
                                  act_hi[:, 0, :, :].bitcast(F32), ALU.subtract).then_inc(actT_ready, 1)

            gathered_lo()

            def item(i):
                split_to(U0 + 3)
                scatter_weights(i)
                for c in range(FC):
                    g = U0 + max(0, 6 * c - 2)
                    split_to(g + 4)
                    if c:
                        item_hidden_lo()
                    if c == 2:
                        add_scattered(1)
                    if c == 3:
                        gather_matrix(i + 2)
                    split_to(g + 6 if c == FC - 1 else g + 7)
                    dve.wait_ge(silu_ready, seen.next(silu_ready))
                    dve.wait_ge(unit_used, seen.at(unit_used, g + 4))
                    dve.tensor_tensor(tokP[:, 0, :], bank[1][:, :], tokA[:, 0, :], ALU.mult).then_inc(act_ready, 1)
                    if c == 1:
                        add_scattered(0)
                gathered_lo()
                split_to(U0 + UI)
                item_hidden_lo()

            n_items = run_items(dve, seen, unit, item)
            scatter_weights(n_items)
            add_scattered(0)
            add_scattered(1)
            seen.item = None
            dve.wait_ge(gain_landed, 16 * (L + 1))
            normalise(row_gain[:, :])

        @block.tensor
        def _(pe):
            seen = Seen(PER_ITEM)

            def product(dst, a_hi, a_lo, b_hi, b_lo, start, stop):
                nc.tensor.matmul(dst, a_hi, b_hi, start=start, stop=False)
                nc.tensor.matmul(dst, a_hi, b_lo, start=False, stop=False)
                return nc.tensor.matmul(dst, a_lo, b_hi, start=False, stop=stop)

            def slab(U, a_hi, a_lo, banks, fresh=None, between=None):
                for j in range(2):
                    pe.wait_ge(lo_ready, seen.at(lo_ready, U + j + 1))
                    s = (U + j) % SPLIT
                    for b, dst in enumerate(banks):
                        for kk in range(4):
                            k = 4 * j + kk
                            if fresh is not None and b == 0:
                                pe.wait_ge(fresh, seen.next(fresh))
                            last = product(dst, a_hi[:, k, b * P:(b + 1) * P], a_lo[:, k, b * P:(b + 1) * P],
                                           w_hi[:, s, kk * N:(kk + 1) * N], w_lo[:, s, kk * N:(kk + 1) * N],
                                           k == 0, k == KD - 1)
                    last.then_inc(unit_used, 1)
                    if j == 0 and between is not None:
                        between()

            def rows(U, units, a_hi, a_lo, blocks, first_bank, start, stop):
                for j in range(units):
                    pe.wait_ge(lo_ready, seen.at(lo_ready, U + j + 1))
                    s = (U + j) % SPLIT
                    for b in range(blocks):
                        for kk in range(2):
                            for h in range(2):
                                w = slice(kk * D + h * N, kk * D + (h + 1) * N)
                                last = product(bank[first_bank + 2 * b + h][:, :], a_hi(2 * j + kk, b), a_lo(2 * j + kk, b),
                                               w_hi[:, s, w], w_lo[:, s, w], start and j == 0 and kk == 0,
                                               stop and j == units - 1 and kk == 1)
                    last.then_inc(unit_used, 1)

            def transpose_x(source, ready):
                pe.wait_ge(ready, seen.next(ready, TB))
                for k in range(KD):
                    for b in range(TB):
                        last = nc.tensor.transpose(bank[4 + k // 2][:, (k % 2) * S + b * P:(k % 2) * S + (b + 1) * P],
                                                   source[:, b, k * P:(k + 1) * P], ident[:, :])
                    if k % 2:
                        last.then_inc(xT_done, 1)

            def transpose_half(source, ready, first_bank, done):
                pe.wait_ge(ready, seen.next(ready, TB))
                for c in range(CC):
                    for b in range(TB):
                        last = nc.tensor.transpose(bank[first_bank + c // 2][:, (c % 2) * S + b * P:(c % 2) * S + (b + 1) * P],
                                                   source[:, b, c * P:(c + 1) * P], ident[:, :])
                    if c % 2:
                        last.then_inc(done, 1)

            low, high = [bank[0][:, :], bank[1][:, :]], [bank[2][:, :], bank[3][:, :]]

            def mixer(l, U):
                transpose_x(xn, xn_ready)
                slab(U, hT_hi, hT_lo, low, fresh=hT_ready)
                slab(U + 2, hT_hi, hT_lo, high)
                pe.wait_ge(sig_ready, seen.next(sig_ready, TB))
                slab(U + 4, hT_hi, hT_lo, low)
                transpose_half(tokA, u_ready, 4, uT_done)
                slab(U + 6, hT_hi, hT_lo, high)
                transpose_half(tokP, p_ready, 6, pT_done)
                slab(U + 8, hT_hi, hT_lo, low)
                pe.wait_ge(gates_ready, seen.next(gates_ready, TB))
                slab(U + 10, hT_hi, hT_lo, high)
                pe.wait_ge(gates_ready, seen.next(gates_ready, TB))
                slab(U + 12, hT_hi, hT_lo, low)
                pe.wait_ge(conv_ready, seen.next(conv_ready))
                for c in range(CC):
                    last = nc.tensor.matmul(bank[4][:, 0:S], mean_w[:, :], conv[:, c, :], start=c == 0, stop=c == CC - 1)
                last.then_inc(mean_done, 1)
                pe.wait_ge(gates_ready, seen.next(gates_ready, 2 * TB))
                pe.wait_ge(dT_ready, seen.next(dT_ready, GROUPS))
                pe.wait_ge(lo_ready, seen.at(lo_ready, U + 15))
                s = (U + 14) % SPLIT
                for b in range(TB):
                    for g in range(GROUPS):
                        a = slice(g * S + b * P, g * S + (b + 1) * P)
                        w = slice(g * GO, (g + 1) * GO)
                        last = product(bank[2 * b + g // 2][:, (g % 2) * GO:(g % 2 + 1) * GO], dT_hi[:, a], dT_lo[:, a],
                                       w_hi[:, s, w], w_lo[:, s, w], True, True)
                last.then_inc(unit_used, 1)
                pe.wait_ge(centred_sq, seen.next(centred_sq))
                for c in range(CC):
                    last = nc.tensor.matmul(bank[5][:, 0:S], mean_w[:, :], sq[:, c * S:(c + 1) * S], start=c == 0, stop=c == CC - 1)
                last.then_inc(var_done, 1)
                pe.wait_ge(cT_ready, seen.next(cT_ready, CC))
                pe.wait_ge(yp_merged, seen.next(yp_merged, 2 * TB))
                cols = lambda t: (lambda k, b: t[:, k * S + b * P:k * S + (b + 1) * P])
                rows(U + 15, 2, cols(cT_hi), cols(cT_lo), TB, 0, True, True)
                transpose_x(gate_c, merged_ready)
                pe.wait_ge(hT_ready, seen.next(hT_ready, KD))
                cols = lambda t: (lambda k, b: t[:, k, b * P:(b + 1) * P])
                rows(U + 17, 4, cols(hT_hi), cols(hT_lo), TB, 0, True, True)

            def hidden_transposes(blocks, n, banks):
                for b in range(blocks):
                    pe.wait_ge(act_ready, seen.next(act_ready))
                    for f in range(n):
                        last = nc.tensor.transpose(bank[banks + b][:, f * P:(f + 1) * P], tokP[:, b, f * P:(f + 1) * P], ident[:, :])
                    last.then_inc(actT_landed, 1)

            hidden = lambda t: (lambda f, b: t[:, b, f, :])

            pe.wait_ge(vecs_landed, 16 * 7)
            pe.wait_ge(consts_ready, 1)
            nc.tensor.transpose(bank[0][:, 0:56], vec_rows[0:56, :], ident[0:56, 0:56]).then_inc(vecT_done, 1)
            for l in range(L):
                nc.tensor.transpose(bank[1 + l][:, 0:124], tap_rows[0:124, l, :], ident[0:124, 0:124]).then_inc(vecT_done, 1)
            pe.wait_ge(vecs_ready, 3)
            mixer(0, 0)

            U = MIXER
            transpose_x(xn, xn_ready)
            for c in range(DC + 1):
                g = U + max(0, 6 * c - 2)
                if c:
                    pe.wait_ge(silu_ready, seen.at(silu_ready, TB * c))
                slab(g, hT_hi, hT_lo, low, fresh=hT_ready if c == 0 else None,
                     between=(lambda: hidden_transposes(TB, 4, 2)) if c else None)
                if c < DC:
                    if c:
                        pe.wait_ge(actT_ready, seen.next(actT_ready, TB))
                    slab(g + 2, hT_hi, hT_lo, high)
                else:
                    pe.wait_ge(actT_ready, seen.next(actT_ready, TB))
                if c:
                    rows(g + (4 if c < DC else 2), 2, hidden(act_hi), hidden(act_lo), TB, 4, c == 1, False)
            hidden_transposes(TB, 2, 2)
            pe.wait_ge(actT_ready, seen.next(actT_ready, TB))
            rows(U + 32, 1, hidden(act_hi), hidden(act_lo), TB, 4, False, True)

            mixer(1, MIXER + 33)

            transpose_x(xn, xn_ready)
            pe.wait_ge(hT_ready, seen.next(hT_ready, KD))
            pe.wait_ge(rw_landed, 16)
            for b in range(TB):
                for k in range(KD):
                    for part in (hT_hi, hT_lo):
                        last = nc.tensor.matmul(bank[0][:, b * E:(b + 1) * E], part[:, k, b * P:(b + 1) * P].bitcast(F32),
                                                rw[:, k, :], start=k == 0 and part is hT_hi, stop=k == KD - 1 and part is hT_lo)
            last.then_inc(logits_done, 1)
            pe.wait_ge(consts_ready, 2)
            pe.wait_ge(mask_ready, seen.next(mask_ready))
            mask = lambda b: route[:, 6, b, :]
            nc.tensor.matmul(bank[3][:, 0:E], before[:, :], mask(0), start=True, stop=True)
            nc.tensor.matmul(bank[3][:, E:2 * E], ones[:, :], mask(0), start=True, stop=False)
            nc.tensor.matmul(bank[3][:, E:2 * E], before[:, :], mask(1), start=False, stop=True)
            nc.tensor.matmul(bank[3][:, 2 * E:3 * E], ones[:, :], mask(0), start=True, stop=False)
            nc.tensor.matmul(bank[3][:, 2 * E:3 * E], ones[:, :], mask(1), start=False, stop=True).then_inc(rank_done, 1)

            def gather():
                pe.wait_ge(onehot_ready, seen.next(onehot_ready))
                for k in range(KD):
                    for b in range(TB):
                        last = nc.tensor.matmul(bank[6 + k // 4][:, (k % 4) * P:(k % 4 + 1) * P], xn[:, b, k * P:(k + 1) * P],
                                                onehot[:, b, :], start=b == 0, stop=b == TB - 1)
                    if k % 4 == 3:
                        last.then_inc(gather_done, 1)

            def spread_transposes():
                pe.wait_ge(spread_ready, seen.next(spread_ready))
                for b in range(TB):
                    last = nc.tensor.transpose(bank[3][:, b * P:(b + 1) * P], spread[:, b, :], ident[:, :])
                last.then_inc(spreadT_landed, 1)

            def scatter(b):
                if b == 0:
                    pe.wait_ge(spreadT_ready, seen.next(spreadT_ready))
                    pe.wait_ge(y_ready, seen.next(y_ready))
                for h in range(2):
                    if b:
                        pe.wait_ge(scatter_added, seen.next(scatter_added))
                    nc.tensor.matmul(bank[6 + h][:, :], spreadT[:, b, :], y[:, h * N:(h + 1) * N],
                                     start=True, stop=True).then_inc(scatter_done, 1)

            gather()
            dense_silu = TB * (DC + 1)

            def item(i):
                for c in range(FC):
                    g = U0 + max(0, 6 * c - 2)
                    if c:
                        pe.wait_ge(silu_ready, seen.at(silu_ready, dense_silu + c))
                    slab(g, tokT_hi, tokT_lo, low[:1], fresh=tokT_ready if c == 0 else None,
                         between=(lambda: hidden_transposes(1, 4, 2)) if c else None)
                    slab(g + 2, tokT_hi, tokT_lo, low[1:])
                    if c == 0:
                        spread_transposes()
                    if c == 1:
                        scatter(0)
                    if c == 4:
                        pe.wait_ge(scatter_added, seen.next(scatter_added, 2))
                        gather()
                    if c:
                        pe.wait_ge(actT_ready, seen.next(actT_ready))
                        rows(g + 4, 2, hidden(act_hi), hidden(act_lo), 1, 4, c == 1, False)
                    if c == 1:
                        scatter(1)
                hidden_transposes(1, 4, 2)
                pe.wait_ge(actT_ready, seen.next(actT_ready))
                rows(U0 + UI - 2, 2, hidden(act_hi), hidden(act_lo), 1, 4, False, True)

            run_items(pe, seen, [0], item)
            spread_transposes()
            scatter(0)
            scatter(1)


_INS = ["x", "mix_norm", "w_in", "conv_dw", "conv_dw_b", "conv_ln_g", "conv_ln_b", "w_conv_out", "w_pool", "pool_scale",
        "w_out", "ffn_norm", "dense_w_gate", "dense_w_up", "dense_w_down", "router_w", "moe_w_gate", "moe_w_up",
        "moe_w_down", "final_norm"]
_OUTS = [((1, 256, 1024), "float32")]


def kernel(**inputs):
    import numpy as _np
    import concourse.bacc as _bacc
    from concourse import mybir as _mybir
    from concourse.bass_utils import run_bass_kernel_spmd as _run

    nc = _bacc.Bacc("TRN2", target_bir_lowering=False, num_devices=1)
    arrays, args = {}, []
    for name in _INS:
        a = _np.ascontiguousarray(inputs[name])
        arrays[f"in_{name}_dram"] = a
        args.append(nc.dram_tensor(f"in_{name}_dram", a.shape, _mybir.dt.from_np(a.dtype), kind="ExternalInput").ap())
    for i, (shape, dtype) in enumerate(_OUTS):
        dt = _mybir.dt.from_np(_np.dtype(dtype))
        args.append(nc.dram_tensor(f"out_{i}_dram", shape, dt, kind="ExternalOutput").ap())
    trunk_kernel(nc, *args)
    r = _run(nc, [arrays], core_ids=[0])
    return r.results[0]["out_0_dram"]
```

```python
from contextlib import ExitStack

import concourse.bass as bass
from concourse import mybir

ALU = mybir.AluOpType
ACT = mybir.ActivationFunctionType
AX_X = mybir.AxisListType.X
F32 = mybir.dt.float32
F32R = mybir.dt.float32r
I32 = mybir.dt.int32

P = 128
UNIT = 2048
RAW = 7
RMS_EPS, LN_EPS = 1e-6, 1e-5
SPLIT = 3
OVER = 3
TABLE = 1 + 8 + OVER + 1
NOWHERE = -1000.0


class Seen:

    def __init__(self, per_item):
        self.per_item, self.n, self.item = per_item, {}, None

    def at(self, sem, n):
        per = self.per_item.get(sem.name, 0)
        return n if self.item is None or not per else self.item * per + n

    def next(self, sem, step=1):
        self.n[sem.name] = self.n.get(sem.name, 0) + step
        return self.at(sem, self.n[sem.name])


def trunk_kernel(nc, x, mix_norm, w_in, conv_dw, conv_dw_b, conv_ln_g, conv_ln_b, w_conv_out, w_pool, pool_scale,
                 w_out, ffn_norm, dense_w_gate, dense_w_up, dense_w_down, router_w, moe_w_gate, moe_w_up,
                 moe_w_down, final_norm, out):
    _, S, D = x.shape
    L = w_in.shape[0]
    TAPS, CD = conv_dw.shape[1:]
    GROUPS, GD, GO = w_pool.shape[1:]
    FD = dense_w_gate.shape[2]
    E, _, FE = moe_w_gate.shape[1:]
    TB = S // P
    KD = D // P
    CC = CD // P
    N = 512
    PAD = TAPS - 1
    WINDOWS = (2, 4, 8, 16)
    PRODS = 8
    TV = 15
    PRODUCTS = sorted([(j, CC - 1, j) for j in range(TAPS)] + [(2 * (j - TV) + 1, CC - 2, j) for j in range(TV, TAPS)])
    PRODUCTS = [(c, j) for _, c, j in PRODUCTS]
    ADDS, PRODUCT_USED, first_of, last_add = [], [0] * len(PRODUCTS), {}, {}
    for n, (c, j) in enumerate(PRODUCTS):
        if c not in first_of:
            first_of[c] = n
            continue
        fresh_one = first_of[c] if c not in last_add else None
        ADDS.append((c, fresh_one, n, last_add.get(c)))
        last_add[c] = PRODUCT_USED[n] = len(ADDS)
        if fresh_one is not None:
            PRODUCT_USED[fresh_one] = len(ADDS)
    CONV_STEPS = 2 * TAPS + TV + 1
    FC = FE // N
    DC = FD // N
    assert (TB, KD, CC, GROUPS, FC, DC, FD - DC * N) == (2, 8, 4, 4, 7, 5, 256) and L == 2

    k_rows = lambda w: w.rearrange("(k p) n -> p k n", p=P)

    def slab_units(w, c):
        return [(4, N, lambda j=j: k_rows(w)[:, 4 * j:4 * j + 4, c:c + N]) for j in range(2)]

    def row_units(w, r0, blocks):
        return [(2, D, lambda j=j: k_rows(w)[:, r0 + j:r0 + j + 2, :]) for j in range(0, blocks, 2)]

    def mixer_units(l):
        columns = (CD, 0, 2 * CD) + tuple(3 * CD + N * j for j in range(4))
        units = [u for c in columns for u in slab_units(w_in[l], c)]
        units.append((GROUPS, GO, lambda: w_pool[l].rearrange("g c o -> c g o")))
        return units + row_units(w_conv_out[l], 0, CC) + row_units(w_out[l], 0, KD)

    def dense_units():
        g, u, d = dense_w_gate[0], dense_w_up[0], dense_w_down[0]
        units = []
        for c in range(DC):
            units += slab_units(g, c * N) + slab_units(u, c * N)
            if c:
                units += row_units(d, (c - 1) * 4, 4)
        half = [(4, N, (lambda j=j: k_rows(g)[:, 4 * j:4 * j + 4, DC * N:FD],
                        lambda j=j: k_rows(u)[:, 4 * j:4 * j + 4, DC * N:FD])) for j in range(2)]
        return units + half + row_units(d, (DC - 1) * 4, 4) + row_units(d, DC * 4, 2)

    MIXER = 2 * 7 + 1 + 2 + 4
    STREAM = mixer_units(0) + dense_units() + mixer_units(1)
    U0 = len(STREAM)
    UI = FC * 6
    assert U0 == 2 * MIXER + 33 and U0 % SPLIT == 0 and UI % SPLIT == 0 and UI % RAW == 0

    def item_units(e):
        one = lambda w: w[0, bass.ds(e, 1)].rearrange("a r n -> (a r) n")
        g, u, d = one(moe_w_gate), one(moe_w_up), one(moe_w_down)
        units = []
        for c in range(FC):
            units += slab_units(g, c * N) + slab_units(u, c * N)
            if c:
                units += row_units(d, (c - 1) * 4, 4)
        return units + row_units(d, (FC - 1) * 4, 4)

    unit_width = lambda n: UNIT if n >= U0 else STREAM[n][0] * STREAM[n][1]

    PER_ITEM = dict(hi_ready=UI, lo_ready=UI, unit_used=UI, silu_ready=FC, act_ready=FC,
                    actT_landed=FC, actT_hi=FC, actT_ready=FC, y_ready=1, onehot_ready=1,
                    spread_ready=1, spreadT_landed=1, spreadT_ready=1, scatter_done=4, scatter_added=4, gather_done=2,
                    tokT_hi_ready=KD, tokT_ready=KD)
    landed_at, so_far = [], [0] * RAW
    for n in range(U0 + UI):
        so_far[n % RAW] += 32 if n < U0 and isinstance(STREAM[n][2], tuple) else 16
        landed_at.append(so_far[n % RAW])
    for slot in range(RAW):
        PER_ITEM[f"raw_landed{slot}"] = 16 * UI // RAW

    with ExitStack() as ctx:
        def sb(name, shape, dt=F32):
            return ctx.enter_context(nc.sbuf_tensor(name, shape, dt))

        def sem(name):
            return ctx.enter_context(nc.semaphore(name))

        raw = sb("raw", [P, RAW, UNIT])
        w_hi = sb("w_hi", [P, SPLIT, UNIT], F32R)
        w_lo = sb("w_lo", [P, SPLIT, UNIT], F32R)
        xs = sb("xs", [P, TB, D])
        xn = sb("xn", [P, TB, D])
        hT_hi = sb("hT_hi", [P, KD, S], F32R)
        hT_lo = sb("hT_lo", [P, KD, S], F32R)
        tokA = sb("tokA", [P, TB, N])
        tokP = sb("tokP", [P, TB, N])
        uT = sb("uT", [P, CC, PAD + S])
        band_0 = sb("band_0", [P, GROUPS, S])
        band_1 = sb("band_1", [P, GROUPS, P])
        tap_prod = sb("tap_prod", [P, PRODS, S])
        conv = xn[:, 0, :].rearrange("p (c t) -> p c t", c=CC)
        gate_c = sb("gate_c", [P, TB, D])
        gate_p = sb("gate_p", [P, TB, D])
        cT_hi = sb("cT_hi", [P, CC * S], F32R)
        cT_lo = sb("cT_lo", [P, CC * S], F32R)
        dT_hi = sb("dT_hi", [P, GROUPS * S], F32R)
        dT_lo = sb("dT_lo", [P, GROUPS * S], F32R)
        row_gain = sb("row_gain", [P, D])
        ident = sb("ident", [P, P])
        ones = sb("ones", [P, P])
        mean_w = sb("mean_w", [P, P])
        before = sb("before", [P, P])
        slot_no = sb("slot_no", [P, P])
        vecs = sb("vecs", [P, 56])
        taps = sb("taps", [P, 2, 124])
        small = sb("small", [P, 16])
        rw = sb("rw", [P, KD, E])
        route = sb("route", [P, 16, TB, E])
        rev = sb("rev", [P, TB, E])
        over = sb("over", [P, 8, E])
        pair = sb("pair", [P, 12, TB])
        slot_of = sb("slot_of", [P, TABLE * TB])
        comb_of = sb("comb_of", [P, TABLE * TB])
        items = sb("items", [P, 8], I32)
        onehot, spread, spreadT = (uT[:, c, 0:TB * P].rearrange("p (b t) -> p b t", b=TB) for c in range(3))
        vec_rows = xn[:, 0, 0:P]
        tap_rows = xn[:, 0, P:3 * P].rearrange("p (l c) -> p l c", l=L)
        slot_int = tap_prod[:, 0, 0:P].bitcast(I32)
        sq, junk, y = xn[:, 1, :], gate_c[:, 0, :], gate_p[:, 0, :]
        ln_std, ln_rstd = sq[:, 0:S], sq[:, S:2 * S]
        act_hi = cT_hi[:, :].rearrange("p (b f t) -> p b f t", b=TB, f=4)
        act_lo = cT_lo[:, :].rearrange("p (b f t) -> p b f t", b=TB, f=4)
        tokT_hi = dT_hi[:, :].rearrange("p (k t) -> p k t", k=KD)
        tokT_lo = dT_lo[:, :].rearrange("p (k t) -> p k t", k=KD)
        bank = [ctx.enter_context(nc.psum_tensor(f"bank{i}", [P, N], F32)) for i in range(8)]

        raw_landed = [sem(f"raw_landed{i}") for i in range(RAW)]
        hi_ready, lo_ready, unit_used = sem("hi_ready"), sem("lo_ready"), sem("unit_used")
        x_landed = [sem(f"x_landed{h}") for h in range(2)]
        vecs_landed, rw_landed = sem("vecs_landed"), sem("rw_landed")
        gain_landed, consts_ready, pool_step = sem("gain_landed"), sem("consts_ready"), sem("pool_step")
        vecT_done, vecs_ready = sem("vecT_done"), sem("vecs_ready")
        result_ready, out_stored = sem("result_ready"), sem("out_stored")
        sumsq_ready, meansq_ready, rstd_ready = sem("sumsq_ready"), sem("meansq_ready"), sem("rstd_ready")
        xn_ready, xT_done, hT_hi_ready, hT_ready = sem("xn_ready"), sem("xT_done"), sem("hT_hi_ready"), sem("hT_ready")
        x_ready, dve_step = sem("x_ready"), sem("dve_step")
        left_done = sem("left_done")
        sig_ready, u_ready, p_ready = sem("sig_ready"), sem("u_ready"), sem("p_ready")
        gates_ready, gate_p_scaled = sem("gates_ready"), sem("gate_p_scaled")
        uT_done, uT_ready, conv_step = sem("uT_done"), sem("uT_ready"), sem("conv_step")
        prod_ready, prod_added = sem("prod_ready"), sem("prod_added")
        pooled_done, dT_hi_ready, dT_ready = sem("pooled_done"), sem("dT_hi_ready"), sem("dT_ready")
        mean_done, centred, centred_sq, var_done = sem("mean_done"), sem("centred"), sem("centred_sq"), sem("var_done")
        std_ready, normed, silu_conv = sem("std_ready"), sem("normed"), sem("silu_conv")
        cT_hi_ready, cT_ready = sem("cT_hi_ready"), sem("cT_ready")
        yp_merged, yc_gated, merged_ready = sem("yp_merged"), sem("yc_gated"), sem("merged_ready")
        silu_ready, act_ready = sem("silu_ready"), sem("act_ready")
        actT_landed, actT_hi, actT_ready = sem("actT_landed"), sem("actT_hi"), sem("actT_ready")
        y_ready = sem("y_ready")
        logits_done, diff_ready, probs_ready = sem("logits_done"), sem("diff_ready"), sem("probs_ready")
        mask_ready, rank_done, tables_ready = sem("mask_ready"), sem("rank_done"), sem("tables_ready")
        onehot_ready, gather_done = sem("onehot_ready"), sem("gather_done")
        tokT_hi_ready, tokT_ready = sem("tokT_hi_ready"), sem("tokT_ready")
        spread_ready, spreadT_landed, spreadT_ready = sem("spread_ready"), sem("spreadT_landed"), sem("spreadT_ready")
        scatter_done, scatter_added = sem("scatter_done"), sem("scatter_added")

        X_BANKS, MERGED_BANKS = (4, 6, 5, 7), (0, 2, 1, 3)
        V_MIX, V_FFN, V_CB, V_LG, V_LB = 0, 16, 32, 40, 48

        block = ctx.enter_context(nc.Block())


        @block.sync
        def _(sp):
            seen = Seen(PER_ITEM)

            def load(n, unit):
                blocks, width, source = unit
                if n >= RAW:
                    sp.wait_ge(lo_ready, seen.at(lo_ready, n - RAW + 1))
                dst = raw[:, n % RAW, 0:blocks * width].rearrange("p (k n) -> p k n", k=blocks)
                if isinstance(source, tuple):
                    half = width // 2
                    sp.dma_start(dst[:, :, 0:half], source[0]()).then_inc(raw_landed[n % RAW], 16)
                    sp.dma_start(dst[:, :, half:], source[1]()).then_inc(raw_landed[n % RAW], 16)
                else:
                    sp.dma_start(dst, source()).then_inc(raw_landed[n % RAW], 16)

            def load_x(h):
                half = slice(h * N, (h + 1) * N)
                sp.dma_start(xs[:, :, half], x[0].rearrange("(b p) d -> p b d", p=P)[:, :, half]).then_inc(x_landed[h], 16)

            rows = 0
            for v, per in ((mix_norm, KD), (ffn_norm, KD), (conv_dw_b, CC), (conv_ln_g, CC), (conv_ln_b, CC)):
                sp.dma_start(vec_rows[rows:rows + L * per, :], v.rearrange("l (k p) -> (l k) p", p=P)).then_inc(vecs_landed, 16)
                rows += L * per
            load_x(0)
            for l in range(L):
                sp.dma_start(tap_rows[0:TAPS * CC, l, :], conv_dw[l].rearrange("j (c p) -> (j c) p", p=P)).then_inc(vecs_landed, 16)
            load_x(1)
            for n, unit in enumerate(STREAM):
                load(n, unit)
            with sp.Fori(0, E) as i:
                seen.item = i
                for j, unit in enumerate(item_units(i)):
                    load(U0 + j, unit)
            seen.item = None
            sp.wait_ge(tables_ready, 2)
            n_items = sp.value_load(items[0:1, 0:1], min_val=E, max_val=E + OVER)
            with sp.If(n_items > E):
                with sp.Fori(E, n_items) as i:
                    seen.item = i
                    e = sp.value_load(items[0:1, bass.ds(i - (E - 1), 1)], min_val=0, max_val=E - 1)
                    for j, unit in enumerate(item_units(e)):
                        load(U0 + j, unit)
            for b in range(TB):
                sp.wait_ge(result_ready, b + 1)
                sp.dma_start(out[0, b * P:(b + 1) * P, :], xs[:, b, :]).then_inc(out_stored, 16)
            sp.wait_ge(out_stored, 16 * TB)

        @block.gpsimd
        def _(pool):
            seen = Seen(PER_ITEM)
            steps = [0]

            def step(ins):
                steps[0] += 1
                ins.then_inc(pool_step, 1)
                pool.wait_ge(pool_step, steps[0])

            step(pool.memset(ident[:, :], 0.0))
            step(pool.affine_select(out=ident[:, :], in_=ident[:, :], compare_op=ALU.not_equal, fill=1.0, base=0,
                                    pattern=[[-1, P]], channel_multiplier=1))
            pool.memset(small[:, 4:6], -0.5)
            pool.memset(small[:, 13:14], LN_EPS)
            pool.memset(uT[:, :, 0:PAD], 0.0)
            step(pool.memset(mean_w[:, :], 1.0 / CD))
            pool.memset(small[:, 12:13], 0.0).then_inc(consts_ready, 1)

            def inverse_root():
                pool.wait_ge(meansq_ready, seen.next(meansq_ready))
                pool.tensor_tensor(small[:, 6:8], small[:, 2:4], small[:, 4:6], ALU.pow).then_inc(rstd_ready, 1)

            inverse_root()
            for g, w in enumerate(WINDOWS):
                pool.memset(band_0[:, g, w - 1:S], 1.0 / w)
                for t in range(w - 1):
                    pool.memset(band_0[:, g, t:t + 1], 1.0 / (t + 1))
                step(pool.memset(band_1[:, g, :], 1.0 / w))
                for band, cols in ((band_0, S), (band_1, P)):
                    step(pool.affine_select(out=band[:, g, :], in_=band[:, g, :], compare_op=ALU.is_ge, fill=0.0, base=0,
                                            pattern=[[1, cols]], channel_multiplier=-1))
                    step(pool.affine_select(out=band[:, g, :], in_=band[:, g, :], compare_op=ALU.is_ge, fill=0.0,
                                            base=w - 1, pattern=[[-1, cols]], channel_multiplier=1))
                    step(pool.tensor_tensor(band[:, g, 0:P], band[:, g, 0:P], ident[:, :], ALU.subtract))
            pool.memset(small[:, 12:13], 0.0).then_inc(consts_ready, 1)

            def router_constants():
                step(pool.memset(ones[:, :], 1.0))
                step(pool.affine_select(out=before[:, :], in_=ones[:, :], compare_op=ALU.is_gt, fill=0.0, base=0,
                                        pattern=[[1, P]], channel_multiplier=-1))
                step(pool.iota(slot_int, pattern=[[1, P]], base=0, channel_multiplier=0))
                step(pool.tensor_copy(slot_no[:, :], slot_int))
                for e in range(E):
                    pool.memset(rev[:, :, e:e + 1], float(E - e))
                pool.memset(slot_of[:, :], NOWHERE)
                step(pool.memset(comb_of[:, :], 0.0))
                pool.memset(small[:, 12:13], 0.0).then_inc(consts_ready, 1)

            for l in range(L):
                for c, first, n, before_this in ADDS:
                    pool.wait_ge(prod_ready, len(PRODUCTS) * l + n + 1)
                    if before_this:
                        pool.wait_ge(prod_added, len(ADDS) * l + before_this)
                    part = conv[:, c, :] if first is None else tap_prod[:, (len(PRODUCTS) * l + first) % PRODS, :]
                    pool.tensor_tensor(conv[:, c, :], part, tap_prod[:, (len(PRODUCTS) * l + n) % PRODS, :],
                                       ALU.add).then_inc(prod_added, 1)
                pool.wait_ge(gain_landed, seen.next(gain_landed, 16))
                pool.wait_ge(gates_ready, seen.next(gates_ready, 2 * TB))
                for h in range(2):
                    for b in range(TB):
                        pool.wait_ge(gates_ready, seen.next(gates_ready))
                        part = gate_p[:, b, h * N:(h + 1) * N]
                        pool.tensor_tensor(part, part, row_gain[:, h * N:(h + 1) * N], ALU.mult).then_inc(gate_p_scaled, 1)
                inverse_root()
                if l == 0:
                    router_constants()
                    inverse_root()
            inverse_root()

        def run_items(eng, seen, unit, item):
            base = dict(seen.n)
            with eng.Fori(0, E) as i:
                seen.item, unit[0] = i, U0
                item(i)
            seen.item = None
            eng.wait_ge(tables_ready, 2)
            n_items = eng.value_load(items[0:1, 0:1], min_val=E, max_val=E + OVER)
            for name, n in seen.n.items():
                assert n - base.get(name, 0) == (PER_ITEM[name] if n != base.get(name, 0) else 0), name
            with eng.If(n_items > E):
                with eng.Fori(E, n_items) as i:
                    seen.n = dict(base)
                    seen.item, unit[0] = i, U0
                    item(i)
            seen.n, seen.item = dict(base), n_items
            return n_items

        @block.scalar
        def _(act):
            seen = Seen(PER_ITEM)
            unit = [0]

            def split_to(n):
                while unit[0] < n:
                    u = unit[0]
                    act.wait_ge(raw_landed[u % RAW], seen.at(raw_landed[u % RAW], landed_at[u]))
                    if u >= SPLIT:
                        act.wait_ge(unit_used, seen.at(unit_used, u - SPLIT + 1))
                    width = unit_width(u)
                    act.activation(w_hi[:, u % SPLIT, 0:width], raw[:, u % RAW, 0:width], ACT.Copy).then_inc(hi_ready, 1)
                    unit[0] += 1

            def rstd(b):
                return small[:, 6 + b:7 + b]

            def sums_of_squares():
                for b in range(TB):
                    act.activation(junk, xs[:, b, :], ACT.Square, accum_out=small[:, b:b + 1]).then_inc(sumsq_ready, 1)
                    act.wait_ge(sumsq_ready, seen.next(sumsq_ready))

            def operand(gain, banks):
                for k in range(KD):
                    if k % 2 == 0:
                        act.wait_ge(xT_done, seen.next(xT_done))
                    scale = 1.0 if gain is None else vecs[:, gain + k:gain + k + 1]
                    act.activation(hT_hi[:, k, :], bank[banks[k // 2]][:, (k % 2) * S:(k % 2 + 1) * S], ACT.Copy,
                                   scale=scale).then_inc(hT_hi_ready, 1)

            prods = [0]

            def tap_products(l, n):
                while prods[0] < len(PRODUCTS) * l + n:
                    c, j = PRODUCTS[prods[0] - len(PRODUCTS) * l]
                    if prods[0] >= PRODS:
                        old_l, old = divmod(prods[0] - PRODS, len(PRODUCTS))
                        act.wait_ge(prod_added, len(ADDS) * old_l + PRODUCT_USED[old])
                    tap = taps[:, l, CC * j + c:CC * j + c + 1]
                    bias = vecs[:, V_CB + CC * l + c:V_CB + CC * l + c + 1] if j == 0 else 0.0
                    act.activation(tap_prod[:, prods[0] % PRODS, :], uT[:, c, j:j + S], ACT.Identity, scale=tap,
                                   bias=bias).then_inc(prod_ready, 1)
                    prods[0] += 1

            def gate_half(U, s):
                dst, c = (gate_c, gate_p)[s // 2], (s % 2) * N
                act.wait_ge(unit_used, seen.at(unit_used, U + 8 + 2 * s))
                for b in range(TB):
                    act.activation(dst[:, b, c:c + N], bank[2 * ((s + 1) % 2) + b][:, :], ACT.Sigmoid,
                                   scale=rstd(b)).then_inc(gates_ready, 1)

            def mixer(l, U):
                if l:
                    split_to(U + 2)
                operand(V_MIX + KD * l, X_BANKS)
                split_to(U + 3)
                if l:
                    act.wait_ge(x_ready, seen.next(x_ready, 2 * TB))
                sums_of_squares()
                split_to(U + 5)
                act.wait_ge(unit_used, seen.at(unit_used, U + 2))
                act.wait_ge(rstd_ready, seen.next(rstd_ready))
                for b in range(TB):
                    act.activation(tokA[:, b, :], bank[b][:, :], ACT.Sigmoid, scale=rstd(b)).then_inc(sig_ready, 1)
                split_to(U + 8)
                for j in range(2):
                    act.wait_ge(uT_done, seen.next(uT_done))
                    act.activation(uT[:, 2 * j:2 * j + 2, PAD:], bank[6 + j][:, :].rearrange("p (c t) -> p c t", c=2),
                                   ACT.Copy).then_inc(uT_ready, 1)
                act.wait_ge(uT_ready, seen.next(uT_ready, 2))
                tap_products(l, 6)
                split_to(U + 9)
                act.wait_ge(unit_used, seen.at(unit_used, U + 6))
                for b in range(TB):
                    act.activation(tokP[:, b, :], bank[b][:, :], ACT.Copy, scale=rstd(b)).then_inc(p_ready, 1)
                for s in range(3):
                    tap_products(l, 12 + 14 * s)
                    split_to(U + 10 + 2 * s)
                    if s == 1:
                        for j in range(2):
                            act.wait_ge(pooled_done, seen.next(pooled_done))
                            act.activation(dT_hi[:, 2 * j * S:2 * (j + 1) * S], bank[6 + j][:, :], ACT.Copy).then_inc(dT_hi_ready, 1)
                    tap_products(l, (19, 33, len(PRODUCTS))[s])
                    if s < 2:
                        split_to(U + 11 + 2 * s)
                    gate_half(U, s)
                act.wait_ge(centred, seen.next(centred))
                act.activation(sq, xn[:, 0, :], ACT.Square).then_inc(centred_sq, 1)
                split_to(U + 15)
                act.wait_ge(var_done, seen.next(var_done))
                act.activation(ln_std[:, :], bank[7][:, 0:S], ACT.Sqrt, bias=small[:, 13:14]).then_inc(std_ready, 1)
                split_to(U + 16)
                gate_half(U, 3)
                act.wait_ge(normed, seen.next(normed))
                for c in range(CC):
                    g, b = V_LG + CC * l + c, V_LB + CC * l + c
                    act.activation(conv[:, c, :], conv[:, c, :], ACT.Silu, bias=vecs[:, b:b + 1], scale=vecs[:, g:g + 1]).then_inc(silu_conv, 1)
                for c in range(CC):
                    act.wait_ge(silu_conv, seen.next(silu_conv))
                    act.activation(cT_hi[:, c * S:(c + 1) * S], conv[:, c, :], ACT.Copy).then_inc(cT_hi_ready, 1)
                split_to(U + 19)
                operand(None, MERGED_BANKS)
                split_to(U + 21)
                act.wait_ge(gate_p_scaled, 2 * TB * (l + 1))
                row = pool_scale[l + 1:l + 2, :] if l + 1 < L else final_norm.rearrange("(a d) -> a d", a=1)
                act.dma_start(row_gain[:, :], row.to_broadcast([P, D])).then_inc(gain_landed, 16)

            def silu_of_gate(c, g, width):
                act.wait_ge(unit_used, seen.at(unit_used, g + 2))
                for b in range(TB):
                    if c:
                        act.wait_ge(act_ready, seen.at(act_ready, TB * (c - 1) + b + 1))
                    act.activation(tokA[:, b, 0:width], bank[b][:, 0:width], ACT.Silu, scale=rstd(b)).then_inc(silu_ready, 1)

            def hidden_hi(n):
                for b in range(TB):
                    act.wait_ge(actT_landed, seen.next(actT_landed))
                    act.activation(act_hi[:, b, 0:n, :], bank[2 + b][:, 0:n * P].rearrange("p (f t) -> p f t", f=n),
                                   ACT.Copy).then_inc(actT_hi, 1)

            act.dma_start(row_gain[:, :], pool_scale[0:1, :].to_broadcast([P, D])).then_inc(gain_landed, 16)
            act.dma_start(rw[:, :, :], router_w[0].rearrange("(k p) e -> p k e", p=P)).then_inc(rw_landed, 16)
            for i, (dst, n) in enumerate(((vecs[:, :], 56), (taps[:, 0, :], 124), (taps[:, 1, :], 124))):
                act.wait_ge(vecT_done, seen.next(vecT_done))
                act.activation(dst, bank[i][:, 0:n], ACT.Copy).then_inc(vecs_ready, 1)
            act.wait_ge(vecs_ready, 3)
            act.wait_ge(consts_ready, 1)
            for h in range(2):
                act.wait_ge(x_landed[h], 16)
            mixer(0, 0)

            U = MIXER
            split_to(U + 2)
            operand(V_FFN, X_BANKS)
            split_to(U + 3)
            act.wait_ge(x_ready, seen.next(x_ready, 2 * TB))
            sums_of_squares()
            act.wait_ge(rstd_ready, seen.next(rstd_ready))
            for c in range(DC + 1):
                g = U + max(0, 6 * c - 2)
                split_to(g + 4)
                if c:
                    hidden_hi(4)
                split_to(g + 5)
                silu_of_gate(c, g, N if c < DC else N // 2)
            hidden_hi(2)

            mixer(1, MIXER + 33)

            operand(V_FFN + KD, X_BANKS)
            act.wait_ge(x_ready, seen.next(x_ready, 2 * TB))
            sums_of_squares()
            act.wait_ge(diff_ready, seen.next(diff_ready))
            act.activation(pair[:, 8, :], pair[:, 7, :], ACT.Sigmoid).then_inc(probs_ready, 1)
            act.activation(pair[:, 9, :], pair[:, 7, :], ACT.Sigmoid, scale=-1.0).then_inc(probs_ready, 1)

            def gathered_hi():
                for k in range(KD):
                    if k % 4 == 0:
                        act.wait_ge(gather_done, seen.next(gather_done))
                    g = V_FFN + KD + k
                    act.activation(tokT_hi[:, k, :], bank[6 + k // 4][:, (k % 4) * P:(k % 4 + 1) * P], ACT.Copy,
                                   scale=vecs[:, g:g + 1]).then_inc(tokT_hi_ready, 1)

            def result_of_item():
                act.wait_ge(unit_used, seen.at(unit_used, U0))
                act.activation(y[:, 0:N], bank[4][:, :], ACT.Copy)
                act.activation(y[:, N:], bank[5][:, :], ACT.Copy).then_inc(y_ready, 1)

            def scatter_matrix():
                act.wait_ge(spreadT_landed, seen.next(spreadT_landed))
                act.activation(spreadT[:, :, :], bank[3][:, 0:TB * P].rearrange("p (b t) -> p b t", b=TB),
                               ACT.Copy).then_inc(spreadT_ready, 1)

            def item_hidden_hi(slot=0):
                act.wait_ge(actT_landed, seen.next(actT_landed))
                act.activation(act_hi[:, slot, :, :], bank[2][:, :].rearrange("p (f t) -> p f t", f=4), ACT.Copy).then_inc(actT_hi, 1)

            gathered_hi()
            used_before = TB * (DC + 1)

            def item(i):
                split_to(U0 + 3)
                result_of_item()
                for c in range(FC):
                    g = U0 + max(0, 6 * c - 2)
                    split_to(g + 4)
                    if c:
                        item_hidden_hi()
                    if c == 1:
                        scatter_matrix()
                    split_to(g + 5)
                    act.wait_ge(unit_used, seen.at(unit_used, g + 2))
                    act.wait_ge(act_ready, seen.at(act_ready, used_before + c))
                    act.activation(tokA[:, 0, :], bank[0][:, :], ACT.Silu).then_inc(silu_ready, 1)
                split_to(U0 + UI - 1)
                item_hidden_hi(1)
                split_to(U0 + UI)
                gathered_hi()

            run_items(act, seen, unit, item)
            result_of_item()
            scatter_matrix()
            act.wait_ge(scatter_added, seen.at(scatter_added, 2 * TB))
            sums_of_squares()

        @block.vector
        def _(dve):
            seen = Seen(PER_ITEM)
            unit = [0]
            steps = [0]

            def step(ins):
                steps[0] += 1
                ins.then_inc(dve_step, 1)
                dve.wait_ge(dve_step, steps[0])

            def split_to(n):
                while unit[0] < n:
                    u = unit[0]
                    dve.wait_ge(hi_ready, seen.at(hi_ready, u + 1))
                    width = unit_width(u)
                    dve.tensor_tensor(w_lo[:, u % SPLIT, 0:width], raw[:, u % RAW, 0:width],
                                      w_hi[:, u % SPLIT, 0:width].bitcast(F32), ALU.subtract).then_inc(lo_ready, 1)
                    unit[0] += 1

            def rstd(b):
                return small[:, 6 + b:7 + b]

            def mean_squares():
                dve.wait_ge(sumsq_ready, seen.next(sumsq_ready, TB))
                dve.tensor_scalar(small[:, 2:4], small[:, 0:2], 1.0 / D, RMS_EPS, ALU.mult, ALU.add).then_inc(meansq_ready, 1)

            def operand(gain, banks):
                for k in range(KD):
                    if k % 2 == 0:
                        dve.wait_ge(hT_hi_ready, seen.next(hT_hi_ready, 2))
                    src = bank[banks[k // 2]][:, (k % 2) * S:(k % 2 + 1) * S]
                    scale = 1.0 if gain is None else vecs[:, gain + k:gain + k + 1]
                    dve.scalar_tensor_tensor(hT_lo[:, k, :], src, scale, hT_hi[:, k, :].bitcast(F32),
                                             ALU.mult, ALU.subtract).then_inc(hT_ready, 1)

            conv_steps = [0]
            last_step = {}

            def conv_tap(l, j):
                for c in range(2 if j >= TV else 3):
                    if j:
                        dve.wait_ge(conv_step, last_step[c])
                    tap = taps[:, l, CC * j + c:CC * j + c + 1]
                    src = uT[:, c, j:j + S]
                    acc = bank[4 + c // 2][:, (c % 2) * S:(c % 2 + 1) * S]
                    if j == 0:
                        bias = vecs[:, V_CB + CC * l + c:V_CB + CC * l + c + 1]
                        ins = dve.tensor_scalar(acc, src, tap, bias, ALU.mult, ALU.add)
                    else:
                        dst = acc if j < TAPS - 1 else conv[:, c, :]
                        ins = dve.scalar_tensor_tensor(dst, src, tap, acc, ALU.mult, ALU.add)
                    ins.then_inc(conv_step, 1)
                    conv_steps[0] += 1
                    last_step[c] = conv_steps[0]

            def mixer(l, U):
                if l:
                    split_to(U + 2)
                operand(V_MIX + KD * l, X_BANKS)
                split_to(U + 3)
                mean_squares()
                split_to(U + 6)
                dve.wait_ge(unit_used, seen.at(unit_used, U + 4))
                dve.wait_ge(rstd_ready, seen.next(rstd_ready))
                for b in range(TB):
                    dve.wait_ge(sig_ready, seen.next(sig_ready))
                    dve.scalar_tensor_tensor(tokA[:, b, :], bank[2 + b][:, :], rstd(b), tokA[:, b, :], ALU.mult,
                                             ALU.mult).then_inc(u_ready, 1)
                split_to(U + 8)
                dve.wait_ge(uT_ready, seen.next(uT_ready, 2))
                for j in range(TAPS):
                    if j >= 7 and (j - 7) % 4 == 0:
                        split_to(min(U + 9 + (j - 7) // 4, U + 14))
                    if j == 20:
                        for i in range(2):
                            dve.wait_ge(dT_hi_ready, seen.next(dT_hi_ready))
                            part = slice(2 * i * S, 2 * (i + 1) * S)
                            dve.tensor_tensor(dT_lo[:, part], bank[6 + i][:, :], dT_hi[:, part].bitcast(F32),
                                              ALU.subtract).then_inc(dT_ready, 1)
                    conv_tap(l, j)
                dve.wait_ge(conv_step, last_step[2])
                dve.wait_ge(prod_added, len(ADDS) * (l + 1))
                dve.tensor_tensor(conv[:, 2, :], bank[5][:, 0:S], conv[:, 2, :], ALU.add).then_inc(conv_step, 1)
                conv_steps[0] += 1
                split_to(U + 14)
                dve.wait_ge(mean_done, seen.next(mean_done))
                dve.tensor_tensor(conv[:, :, :], conv[:, :, :], bank[6][:, 0:S].unsqueeze(1).to_broadcast([P, CC, S]),
                                  ALU.subtract).then_inc(centred, 1)
                split_to(U + 15)
                dve.wait_ge(std_ready, seen.next(std_ready))
                step(dve.reciprocal(ln_rstd[:, :], ln_std[:, :]))
                dve.tensor_tensor(conv[:, :, :], conv[:, :, :], ln_rstd[:, :].unsqueeze(1).to_broadcast([P, CC, S]),
                                  ALU.mult).then_inc(normed, 1)
                split_to(U + 16)
                for c in range(CC):
                    dve.wait_ge(cT_hi_ready, seen.next(cT_hi_ready))
                    dve.tensor_tensor(cT_lo[:, c * S:(c + 1) * S], conv[:, c, :], cT_hi[:, c * S:(c + 1) * S].bitcast(F32),
                                      ALU.subtract).then_inc(cT_ready, 1)
                split_to(U + 17)
                dve.wait_ge(gate_p_scaled, seen.next(gate_p_scaled, 2 * TB))
                dve.wait_ge(unit_used, seen.at(unit_used, U + 15))
                for h in range(2):
                    for b in range(TB):
                        part = gate_p[:, b, h * N:(h + 1) * N]
                        dve.tensor_tensor(part, bank[2 * b + h][:, :], part, ALU.mult).then_inc(yp_merged, 1)
                split_to(U + 19)
                for h in range(2):
                    half_done(h, U + 17)
                    for b in range(TB):
                        part = gate_c[:, b, h * N:(h + 1) * N]
                        dve.tensor_tensor(part, bank[4 + 2 * b + h][:, :], part, ALU.mult).then_inc(yc_gated, 1)
                    if h == 0:
                        dve.wait_ge(yp_merged, seen.next(yp_merged, 2 * TB))
                    for b in range(TB):
                        part = slice(h * N, (h + 1) * N)
                        dve.wait_ge(yc_gated, seen.next(yc_gated))
                        dve.tensor_tensor(gate_c[:, b, part], gate_c[:, b, part], gate_p[:, b, part], ALU.add).then_inc(merged_ready, 1)
                operand(None, MERGED_BANKS)
                split_to(U + 23 if l == 0 else U + 21)
                add_to_x(U + 21)

            def half_done(h, units):
                if h == 0:
                    dve.wait_ge(left_done, seen.next(left_done))
                else:
                    dve.wait_ge(unit_used, seen.at(unit_used, units))

            def add_to_x(units):
                for h in range(2):
                    half_done(h, units)
                    for b in range(TB):
                        part = xs[:, b, h * N:(h + 1) * N]
                        dve.tensor_tensor(part, bank[4 + 2 * b + h][:, :], part, ALU.add).then_inc(x_ready, 1)

            def hidden_lo(n):
                for b in range(TB):
                    dve.wait_ge(actT_hi, seen.next(actT_hi))
                    dve.tensor_tensor(act_lo[:, b, 0:n, :], bank[2 + b][:, 0:n * P].rearrange("p (f t) -> p f t", f=n),
                                      act_hi[:, b, 0:n, :].bitcast(F32), ALU.subtract).then_inc(actT_ready, 1)

            dve.wait_ge(vecs_ready, 3)
            mixer(0, 0)

            U = MIXER
            operand(V_FFN, X_BANKS)
            split_to(U + 3)
            mean_squares()
            dve.wait_ge(rstd_ready, seen.next(rstd_ready))
            for c in range(DC + 1):
                g = U + max(0, 6 * c - 2)
                split_to(g + 4)
                if c:
                    hidden_lo(4)
                split_to(min(g + 7, U + 33))
                if c < DC:
                    dve.wait_ge(unit_used, seen.at(unit_used, g + 4))
                for b in range(TB):
                    dve.wait_ge(silu_ready, seen.next(silu_ready))
                    if c < DC:
                        up, width = bank[2 + b][:, :], N
                    else:
                        up, width = bank[b][:, N // 2:], N // 2
                    dve.scalar_tensor_tensor(tokP[:, b, 0:width], up, rstd(b), tokA[:, b, 0:width], ALU.mult,
                                             ALU.mult).then_inc(act_ready, 1)
            hidden_lo(2)
            split_to(U + 35)
            add_to_x(U + 33)

            mixer(1, MIXER + 33)

            operand(V_FFN + KD, X_BANKS)
            mean_squares()
            dve.wait_ge(rstd_ready, seen.next(rstd_ready))

            per_e = lambda v: v.unsqueeze(2).to_broadcast([P, TB, E])
            LG, EQ, CAND, SEL1, LG2, SEL2, MASK, POS, T1, T2, COMB = range(11)
            r = lambda i: route[:, i, :, :]
            dve.wait_ge(consts_ready, 3)
            dve.wait_ge(logits_done, seen.next(logits_done))
            for b in range(TB):
                step(dve.tensor_scalar(route[:, LG, b, :], bank[0][:, b * E:(b + 1) * E], rstd(b), None, ALU.mult))

            def best(values, v, sel):
                step(dve.tensor_reduce(pair[:, v, :], r(values), AX_X, ALU.max))
                step(dve.tensor_tensor(r(EQ), r(values), per_e(pair[:, v, :]), ALU.is_equal))
                step(dve.tensor_tensor(r(CAND), r(EQ), rev[:, :, :], ALU.mult))
                step(dve.tensor_reduce(pair[:, 2, :], r(CAND), AX_X, ALU.max))
                step(dve.tensor_tensor(r(sel), rev[:, :, :], per_e(pair[:, 2, :]), ALU.is_equal))

            best(LG, 0, SEL1)
            step(dve.scalar_tensor_tensor(r(LG2), r(SEL1), -3.0e38, r(LG), ALU.mult, ALU.add))
            best(LG2, 1, SEL2)
            step(dve.tensor_tensor(pair[:, 7, :], pair[:, 0, :], pair[:, 1, :], ALU.subtract))
            dve.memset(small[:, 11:12], 0.0).then_inc(diff_ready, 1)
            step(dve.tensor_tensor(r(MASK), r(SEL1), r(SEL2), ALU.add))
            dve.memset(small[:, 11:12], 0.0).then_inc(mask_ready, 1)
            for b in range(TB):
                dve.tensor_scalar(xn[:, b, :], xs[:, b, :], rstd(b), None, ALU.mult).then_inc(xn_ready, 1)
            dve.wait_ge(probs_ready, seen.next(probs_ready, 2))
            step(dve.tensor_tensor(r(T1), r(SEL1), per_e(pair[:, 8, :]), ALU.mult))
            step(dve.tensor_tensor(r(T2), r(SEL2), per_e(pair[:, 9, :]), ALU.mult))
            dve.wait_ge(rank_done, seen.next(rank_done))
            step(dve.scalar_tensor_tensor(r(POS), bank[3][:, 0:TB * E].rearrange("p (b e) -> p b e", b=TB), -NOWHERE,
                                          r(MASK), ALU.add, ALU.mult))
            table = lambda t, i, n: t[:, i * TB:(i + n) * TB].rearrange("p (i b) -> p b i", b=TB)
            step(dve.tensor_scalar(r(POS), r(POS), NOWHERE, None, ALU.add))
            step(dve.tensor_tensor(r(COMB), r(T1), r(T2), ALU.add))
            step(dve.tensor_copy(table(slot_of, 1, E), r(POS)))
            step(dve.tensor_copy(table(comb_of, 1, E), r(COMB)))
            dve.memset(small[:, 11:12], 0.0).then_inc(tables_ready, 1)

            def gather_matrix(column):
                for b in range(TB):
                    ins = dve.tensor_scalar(onehot[:, b, :], slot_no[:, :], slot_of[:, bass.ds(column * TB + b, 1)], None, ALU.is_equal)
                ins.then_inc(onehot_ready, 1)

            gather_matrix(1)

            OVM, RANK, SELK, PROD, IDX = range(5)
            v = lambda i: over[:, i, :]
            step(dve.tensor_scalar(v(OVM), bank[3][:, TB * E:(TB + 1) * E], float(P), None, ALU.is_gt))
            step(dve.memset(over[:, RANK, 0:1], 0.0))
            for e in range(1, E):
                step(dve.tensor_tensor(over[:, RANK, e:e + 1], over[:, RANK, e - 1:e], over[:, OVM, e - 1:e], ALU.add))
            step(dve.tensor_scalar(v(IDX), rev[:, 0, :], -1.0, float(E), ALU.mult, ALU.add))
            step(dve.tensor_reduce(small[:, 8:9], v(OVM), AX_X, ALU.add))
            step(dve.tensor_scalar(items[:, 0:1], small[:, 8:9], float(E), None, ALU.add))
            for k in range(OVER):
                step(dve.scalar_tensor_tensor(v(SELK), v(RANK), float(k), v(OVM), ALU.is_equal, ALU.mult))
                step(dve.tensor_tensor(v(PROD), v(SELK), v(IDX), ALU.mult))
                step(dve.tensor_reduce(small[:, 8:9], v(PROD), AX_X, ALU.add))
                step(dve.tensor_copy(items[:, 1 + k:2 + k], small[:, 8:9]))
                step(dve.tensor_reduce(small[:, 9:10], v(SELK), AX_X, ALU.add))
                step(dve.tensor_scalar(small[:, 10:11], small[:, 9:10], -NOWHERE - P, NOWHERE, ALU.mult, ALU.add))
                for src, dst, shift in ((POS, slot_of, True), (COMB, comb_of, False)):
                    step(dve.tensor_tensor(r(T1), r(src), v(SELK).unsqueeze(1).to_broadcast([P, TB, E]), ALU.mult))
                    step(dve.tensor_reduce(pair[:, 3, :], r(T1), AX_X, ALU.add))
                    col = dst[:, (1 + E + k) * TB:(2 + E + k) * TB]
                    if shift:
                        step(dve.tensor_scalar(col, pair[:, 3, :], small[:, 10:11], None, ALU.add))
                    else:
                        step(dve.tensor_copy(col, pair[:, 3, :]))
            dve.memset(small[:, 11:12], 0.0).then_inc(tables_ready, 1)

            def gathered_lo():
                for k in range(KD):
                    if k % 4 == 0:
                        dve.wait_ge(tokT_hi_ready, seen.next(tokT_hi_ready, 4))
                    g = V_FFN + KD + k
                    dve.scalar_tensor_tensor(tokT_lo[:, k, :], bank[6 + k // 4][:, (k % 4) * P:(k % 4 + 1) * P],
                                             vecs[:, g:g + 1], tokT_hi[:, k, :].bitcast(F32), ALU.mult,
                                             ALU.subtract).then_inc(tokT_ready, 1)

            def scatter_weights(column):
                for b in range(TB):
                    ins = dve.tensor_scalar(spread[:, b, :], slot_no[:, :], slot_of[:, bass.ds(column * TB + b, 1)],
                                            comb_of[:, bass.ds(column * TB + b, 1)], ALU.is_equal, ALU.mult)
                ins.then_inc(spread_ready, 1)

            def add_scattered(b):
                for h in range(2):
                    dve.wait_ge(scatter_done, seen.next(scatter_done))
                    part = xs[:, b, h * N:(h + 1) * N]
                    dve.tensor_tensor(part, bank[6 + h][:, :], part, ALU.add).then_inc(scatter_added, 1)

            def item_hidden_lo(slot=0):
                dve.wait_ge(actT_hi, seen.next(actT_hi))
                dve.tensor_tensor(act_lo[:, slot, :, :], bank[2][:, :].rearrange("p (f t) -> p f t", f=4),
                                  act_hi[:, slot, :, :].bitcast(F32), ALU.subtract).then_inc(actT_ready, 1)

            gathered_lo()

            def item(i):
                split_to(U0 + 3)
                scatter_weights(i)
                for c in range(FC):
                    g = U0 + max(0, 6 * c - 2)
                    split_to(g + 4)
                    if c:
                        item_hidden_lo()
                    if c == 2:
                        add_scattered(1)
                    if c == 3:
                        gather_matrix(i + 2)
                    split_to(g + 7 if 0 < c < FC - 1 else g + 6)
                    dve.wait_ge(silu_ready, seen.next(silu_ready))
                    dve.wait_ge(unit_used, seen.at(unit_used, g + 4))
                    dve.tensor_tensor(tokP[:, 0, :], bank[1][:, :], tokA[:, 0, :], ALU.mult).then_inc(act_ready, 1)
                    if c == 1:
                        add_scattered(0)
                split_to(U0 + UI - 1)
                item_hidden_lo(1)
                split_to(U0 + UI)
                gathered_lo()

            n_items = run_items(dve, seen, unit, item)
            scatter_weights(n_items)
            add_scattered(0)
            add_scattered(1)
            seen.item = None
            dve.wait_ge(gain_landed, 16 * (L + 1))
            mean_squares()
            dve.wait_ge(rstd_ready, seen.next(rstd_ready))
            for b in range(TB):
                dve.scalar_tensor_tensor(xs[:, b, :], xs[:, b, :], rstd(b), row_gain[:, :], ALU.mult,
                                         ALU.mult).then_inc(result_ready, 1)

        @block.tensor
        def _(pe):
            seen = Seen(PER_ITEM)

            def product(dst, a_hi, a_lo, b_hi, b_lo, start, stop):
                nc.tensor.matmul(dst, a_hi, b_hi, start=start, stop=False)
                nc.tensor.matmul(dst, a_hi, b_lo, start=False, stop=False)
                return nc.tensor.matmul(dst, a_lo, b_hi, start=False, stop=stop)

            def slab(U, a_hi, a_lo, banks, fresh=None, between=None):
                for j in range(2):
                    pe.wait_ge(lo_ready, seen.at(lo_ready, U + j + 1))
                    s = (U + j) % SPLIT
                    for b, dst in enumerate(banks):
                        for kk in range(4):
                            k = 4 * j + kk
                            if fresh is not None and b == 0:
                                pe.wait_ge(fresh, seen.next(fresh))
                            last = product(dst, a_hi[:, k, b * P:(b + 1) * P], a_lo[:, k, b * P:(b + 1) * P],
                                           w_hi[:, s, kk * N:(kk + 1) * N], w_lo[:, s, kk * N:(kk + 1) * N],
                                           k == 0, k == KD - 1)
                    last.then_inc(unit_used, 1)
                    if j == 0 and between is not None:
                        between()

            def rows(U, units, a_hi, a_lo, blocks, first_bank, start, stop, fresh=None, between=None, by_halves=False):
                for j in range(units):
                    pe.wait_ge(lo_ready, seen.at(lo_ready, U + j + 1))
                    s = (U + j) % SPLIT
                    steps = [(kk, b, h) for b in range(blocks) for kk in range(2) for h in range(2)]
                    if by_halves and j == units - 1:
                        steps = sorted(steps, key=lambda t: t[2])
                    for kk, b, h in steps:
                        if fresh is not None and b == 0 and h == 0:
                            pe.wait_ge(fresh, seen.next(fresh))
                        w = slice(kk * D + h * N, kk * D + (h + 1) * N)
                        last = product(bank[first_bank + 2 * b + h][:, :], a_hi(2 * j + kk, b), a_lo(2 * j + kk, b),
                                       w_hi[:, s, w], w_lo[:, s, w], start and j == 0 and kk == 0,
                                       stop and j == units - 1 and kk == 1)
                        if by_halves and j == units - 1 and (kk, b, h) == (1, blocks - 1, 0):
                            last.then_inc(left_done, 1)
                    last.then_inc(unit_used, 1)
                    if j == 0 and between is not None:
                        between()

            def transpose_x(source, banks, waits):
                for k in range(KD):
                    if k % 4 == 0:
                        waits(k // 4)
                    for b in range(TB):
                        last = nc.tensor.transpose(bank[banks[k // 2]][:, (k % 2) * S + b * P:(k % 2) * S + (b + 1) * P],
                                                   source[:, b, k * P:(k + 1) * P], ident[:, :])
                    if k % 2:
                        last.then_inc(xT_done, 1)

            def x_half(h):
                pe.wait_ge(x_ready, seen.next(x_ready, TB))

            def transpose_u():
                pe.wait_ge(u_ready, seen.next(u_ready, TB))
                for c in range(CC):
                    for b in range(TB):
                        last = nc.tensor.transpose(bank[6 + c // 2][:, (c % 2) * S + b * P:(c % 2) * S + (b + 1) * P],
                                                   tokA[:, b, c * P:(c + 1) * P], ident[:, :])
                    if c % 2:
                        last.then_inc(uT_done, 1)

            def pool_windows():
                pe.wait_ge(p_ready, seen.next(p_ready, TB))
                pe.wait_ge(uT_ready, seen.next(uT_ready, 2))
                pe.wait_ge(consts_ready, 2)
                for g in range(GROUPS):
                    dst = bank[6 + g // 2][:, (g % 2) * S:(g % 2 + 1) * S]
                    nc.tensor.matmul(dst, tokP[:, 0, g * GD:(g + 1) * GD], band_0[:, g, :], start=True, stop=False)
                    last = nc.tensor.matmul(dst[:, P:S], tokP[:, 1, g * GD:(g + 1) * GD], band_1[:, g, :], start=False, stop=True)
                    if g % 2:
                        last.then_inc(pooled_done, 1)

            low, high = [bank[0][:, :], bank[1][:, :]], [bank[2][:, :], bank[3][:, :]]

            def mixer(l, U, x_waits):
                transpose_x(xs, X_BANKS, x_waits)
                slab(U, hT_hi, hT_lo, low, fresh=hT_ready)
                slab(U + 2, hT_hi, hT_lo, high)
                pe.wait_ge(sig_ready, seen.next(sig_ready, TB))
                slab(U + 4, hT_hi, hT_lo, low, between=transpose_u)
                slab(U + 6, hT_hi, hT_lo, high)
                pool_windows()
                slab(U + 8, hT_hi, hT_lo, low)
                pe.wait_ge(gates_ready, seen.next(gates_ready, TB))
                slab(U + 10, hT_hi, hT_lo, high)
                pe.wait_ge(dT_ready, seen.next(dT_ready, 2))
                pe.wait_ge(conv_step, CONV_STEPS * (l + 1))
                for c in range(CC):
                    last = nc.tensor.matmul(bank[6][:, 0:S], mean_w[:, :], conv[:, c, :], start=c == 0, stop=c == CC - 1)
                last.then_inc(mean_done, 1)

                def variance():
                    pe.wait_ge(centred_sq, seen.next(centred_sq))
                    for c in range(CC):
                        last = nc.tensor.matmul(bank[7][:, 0:S], mean_w[:, :], sq[:, c * S:(c + 1) * S], start=c == 0, stop=c == CC - 1)
                    last.then_inc(var_done, 1)

                pe.wait_ge(gates_ready, seen.next(gates_ready, TB))
                slab(U + 12, hT_hi, hT_lo, low, between=variance)
                pe.wait_ge(lo_ready, seen.at(lo_ready, U + 15))
                s = (U + 14) % SPLIT
                for b in reversed(range(TB)):
                    pe.wait_ge(gates_ready, seen.next(gates_ready, TB))
                    for g in range(GROUPS):
                        a = slice(g * S + b * P, g * S + (b + 1) * P)
                        w = slice(g * GO, (g + 1) * GO)
                        last = product(bank[2 * b + g // 2][:, (g % 2) * GO:(g % 2 + 1) * GO], dT_hi[:, a], dT_lo[:, a],
                                       w_hi[:, s, w], w_lo[:, s, w], True, True)
                last.then_inc(unit_used, 1)
                pe.wait_ge(cT_ready, seen.next(cT_ready, CC))
                cols = lambda t: (lambda k, b: t[:, k * S + b * P:k * S + (b + 1) * P])
                rows(U + 15, 2, cols(cT_hi), cols(cT_lo), TB, 4, True, True, by_halves=True)
                transpose_x(gate_c, MERGED_BANKS, merged)
                cols = lambda t: (lambda k, b: t[:, k, b * P:(b + 1) * P])
                rows(U + 17, 4, cols(hT_hi), cols(hT_lo), TB, 4, True, True, fresh=hT_ready, by_halves=True)

            def hidden_transposes(blocks, n, banks):
                for b in range(blocks):
                    pe.wait_ge(act_ready, seen.next(act_ready))
                    for f in range(n):
                        last = nc.tensor.transpose(bank[banks + b][:, f * P:(f + 1) * P], tokP[:, b, f * P:(f + 1) * P], ident[:, :])
                    last.then_inc(actT_landed, 1)

            hidden = lambda t: (lambda f, b: t[:, b, f, :])

            def merged(h):
                pe.wait_ge(merged_ready, seen.next(merged_ready, TB))

            def x_loaded(h):
                pe.wait_ge(x_landed[h], 16)

            pe.wait_ge(vecs_landed, 16 * 7)
            pe.wait_ge(consts_ready, 1)
            nc.tensor.transpose(bank[0][:, 0:56], vec_rows[0:56, :], ident[0:56, 0:56]).then_inc(vecT_done, 1)
            for l in range(L):
                nc.tensor.transpose(bank[1 + l][:, 0:124], tap_rows[0:124, l, :], ident[0:124, 0:124]).then_inc(vecT_done, 1)
            pe.wait_ge(vecs_ready, 3)
            mixer(0, 0, x_loaded)

            U = MIXER
            transpose_x(xs, X_BANKS, x_half)
            for c in range(DC + 1):
                g = U + max(0, 6 * c - 2)
                if c:
                    pe.wait_ge(silu_ready, seen.at(silu_ready, TB * c))
                slab(g, hT_hi, hT_lo, low, fresh=hT_ready if c == 0 else None,
                     between=(lambda: hidden_transposes(TB, 4, 2)) if c else None)
                if c < DC:
                    if c:
                        pe.wait_ge(actT_ready, seen.next(actT_ready, TB))
                    slab(g + 2, hT_hi, hT_lo, high)
                else:
                    pe.wait_ge(actT_ready, seen.next(actT_ready, TB))
                if c:
                    rows(g + (4 if c < DC else 2), 2, hidden(act_hi), hidden(act_lo), TB, 4, c == 1, False,
                         between=(lambda: hidden_transposes(TB, 2, 2)) if c == DC else None)
            pe.wait_ge(actT_ready, seen.next(actT_ready, TB))
            rows(U + 32, 1, hidden(act_hi), hidden(act_lo), TB, 4, False, True, by_halves=True)

            mixer(1, MIXER + 33, x_half)

            transpose_x(xs, X_BANKS, x_half)
            pe.wait_ge(hT_ready, seen.next(hT_ready, KD))
            pe.wait_ge(rw_landed, 16)
            for b in range(TB):
                for k in range(KD):
                    for part in (hT_hi, hT_lo):
                        last = nc.tensor.matmul(bank[0][:, b * E:(b + 1) * E], part[:, k, b * P:(b + 1) * P].bitcast(F32),
                                                rw[:, k, :], start=k == 0 and part is hT_hi, stop=k == KD - 1 and part is hT_lo)
            last.then_inc(logits_done, 1)
            pe.wait_ge(consts_ready, 3)
            pe.wait_ge(mask_ready, seen.next(mask_ready))
            mask = lambda b: route[:, 6, b, :]
            nc.tensor.matmul(bank[3][:, 0:E], before[:, :], mask(0), start=True, stop=True)
            nc.tensor.matmul(bank[3][:, E:2 * E], ones[:, :], mask(0), start=True, stop=False)
            nc.tensor.matmul(bank[3][:, E:2 * E], before[:, :], mask(1), start=False, stop=True)
            nc.tensor.matmul(bank[3][:, 2 * E:3 * E], ones[:, :], mask(0), start=True, stop=False)
            nc.tensor.matmul(bank[3][:, 2 * E:3 * E], ones[:, :], mask(1), start=False, stop=True).then_inc(rank_done, 1)

            def gather():
                pe.wait_ge(onehot_ready, seen.next(onehot_ready))
                for k in range(KD):
                    for b in range(TB):
                        last = nc.tensor.matmul(bank[6 + k // 4][:, (k % 4) * P:(k % 4 + 1) * P], xn[:, b, k * P:(k + 1) * P],
                                                onehot[:, b, :], start=b == 0, stop=b == TB - 1)
                    if k % 4 == 3:
                        last.then_inc(gather_done, 1)

            def spread_transposes():
                pe.wait_ge(spread_ready, seen.next(spread_ready))
                for b in range(TB):
                    last = nc.tensor.transpose(bank[3][:, b * P:(b + 1) * P], spread[:, b, :], ident[:, :])
                last.then_inc(spreadT_landed, 1)

            def scatter(b):
                if b == 0:
                    pe.wait_ge(spreadT_ready, seen.next(spreadT_ready))
                    pe.wait_ge(y_ready, seen.next(y_ready))
                for h in range(2):
                    if b:
                        pe.wait_ge(scatter_added, seen.next(scatter_added))
                    nc.tensor.matmul(bank[6 + h][:, :], spreadT[:, b, :], y[:, h * N:(h + 1) * N],
                                     start=True, stop=True).then_inc(scatter_done, 1)

            pe.wait_ge(xn_ready, TB)
            gather()
            dense_silu = TB * (DC + 1)

            def item(i):
                for c in range(FC):
                    g = U0 + max(0, 6 * c - 2)
                    if c:
                        pe.wait_ge(silu_ready, seen.at(silu_ready, dense_silu + c))
                    slab(g, tokT_hi, tokT_lo, low[:1], fresh=tokT_ready if c == 0 else None,
                         between=(lambda: hidden_transposes(1, 4, 2)) if c else None)
                    slab(g + 2, tokT_hi, tokT_lo, low[1:])
                    if c == 0:
                        spread_transposes()
                    if c == 1:
                        scatter(0)
                    if c == 4:
                        pe.wait_ge(scatter_added, seen.next(scatter_added, 2))
                        gather()
                    if c:
                        pe.wait_ge(actT_ready, seen.next(actT_ready))
                        rows(g + 4, 2, hidden(act_hi), hidden(act_lo), 1, 4, c == 1, False,
                             between=(lambda: hidden_transposes(1, 4, 2)) if c == FC - 1 else None)
                    if c == 1:
                        scatter(1)
                pe.wait_ge(actT_ready, seen.next(actT_ready))
                rows(U0 + UI - 2, 2, lambda f, b: act_hi[:, 1, f, :], lambda f, b: act_lo[:, 1, f, :], 1, 4, False, True)

            run_items(pe, seen, [0], item)
            spread_transposes()
            scatter(0)
            scatter(1)


_INS = ["x", "mix_norm", "w_in", "conv_dw", "conv_dw_b", "conv_ln_g", "conv_ln_b", "w_conv_out", "w_pool", "pool_scale",
        "w_out", "ffn_norm", "dense_w_gate", "dense_w_up", "dense_w_down", "router_w", "moe_w_gate", "moe_w_up",
        "moe_w_down", "final_norm"]
_OUTS = [((1, 256, 1024), "float32")]


def kernel(**inputs):
    import numpy as _np
    import concourse.bacc as _bacc
    from concourse import mybir as _mybir
    from concourse.bass_utils import run_bass_kernel_spmd as _run

    nc = _bacc.Bacc("TRN2", target_bir_lowering=False, num_devices=1)
    arrays, args = {}, []
    for name in _INS:
        a = _np.ascontiguousarray(inputs[name])
        arrays[f"in_{name}_dram"] = a
        args.append(nc.dram_tensor(f"in_{name}_dram", a.shape, _mybir.dt.from_np(a.dtype), kind="ExternalInput").ap())
    for i, (shape, dtype) in enumerate(_OUTS):
        dt = _mybir.dt.from_np(_np.dtype(dtype))
        args.append(nc.dram_tensor(f"out_{i}_dram", shape, dt, kind="ExternalOutput").ap())
    trunk_kernel(nc, *args)
    r = _run(nc, [arrays], core_ids=[0])
    return r.results[0]["out_0_dram"]
```

```python
from contextlib import ExitStack

import numpy as np

import concourse.bass as bass
from concourse import mybir

ALU = mybir.AluOpType
ACT = mybir.ActivationFunctionType
AX_X = mybir.AxisListType.X
F32 = mybir.dt.float32
F32R = mybir.dt.float32r
I32 = mybir.dt.int32

P = 128
UNIT = 2048
RAW = 7
RMS_EPS, LN_EPS = 1e-6, 1e-5
SPLIT = 3
OVER = 3
TABLE = 1 + 8 + OVER + 1
NOWHERE = -1000.0


class Seen:

    def __init__(self, per_item):
        self.per_item, self.n, self.item = per_item, {}, None

    def at(self, sem, n):
        per = self.per_item.get(sem.name, 0)
        return n if self.item is None or not per else self.item * per + n

    def next(self, sem, step=1):
        self.n[sem.name] = self.n.get(sem.name, 0) + step
        return self.at(sem, self.n[sem.name])


def trunk_kernel(nc, x, mix_norm, w_in, conv_dw, conv_dw_b, conv_ln_g, conv_ln_b, w_conv_out, w_pool, pool_scale,
                 w_out, ffn_norm, dense_w_gate, dense_w_up, dense_w_down, router_w, moe_w_gate, moe_w_up,
                 moe_w_down, final_norm, out):
    _, S, D = x.shape
    L = w_in.shape[0]
    TAPS, CD = conv_dw.shape[1:]
    GROUPS, GD, GO = w_pool.shape[1:]
    FD = dense_w_gate.shape[2]
    E, _, FE = moe_w_gate.shape[1:]
    TB = S // P
    KD = D // P
    CC = CD // P
    N = 512
    PAD = TAPS - 1
    WINDOWS = (2, 4, 8, 16)
    REACH = max(WINDOWS)
    PRODS = 6
    TP, TV = 16, 19
    PRODUCTS = sorted([(j, CC - 1, j) for j in range(TAPS)] + [(2 * (j - TV) + 1, CC - 2, j) for j in range(TV, TAPS)])
    PRODUCTS = [(c, j) for _, c, j in PRODUCTS]
    ADDS, PRODUCT_USED, first_of, last_add = [], [0] * len(PRODUCTS), {}, {}
    for n, (c, j) in enumerate(PRODUCTS):
        if c not in first_of:
            first_of[c] = n
            continue
        fresh_one = first_of[c] if c not in last_add else None
        ADDS.append((c, fresh_one, n, last_add.get(c)))
        last_add[c] = PRODUCT_USED[n] = len(ADDS)
        if fresh_one is not None:
            PRODUCT_USED[fresh_one] = len(ADDS)
    CONV_STEPS = 2 * TAPS + TV - TP + 1
    FC = FE // N
    DC = FD // N
    assert (TB, KD, CC, GROUPS, FC, DC, FD - DC * N) == (2, 8, 4, 4, 7, 5, 256) and L == 2

    k_rows = lambda w: w.rearrange("(k p) n -> p k n", p=P)

    def slab_units(w, c):
        return [(4, N, lambda j=j: k_rows(w)[:, 4 * j:4 * j + 4, c:c + N]) for j in range(2)]

    def row_units(w, r0, blocks):
        return [(2, D, lambda j=j: k_rows(w)[:, r0 + j:r0 + j + 2, :]) for j in range(0, blocks, 2)]

    def mixer_units(l):
        columns = (CD, 0, 2 * CD) + tuple(3 * CD + N * j for j in range(4))
        units = [u for c in columns for u in slab_units(w_in[l], c)]
        units.append((GROUPS, GO, lambda: w_pool[l].rearrange("g c o -> c g o")))
        return units + row_units(w_conv_out[l], 0, CC) + row_units(w_out[l], 0, KD)

    def dense_units():
        g, u, d = dense_w_gate[0], dense_w_up[0], dense_w_down[0]
        units = []
        for c in range(DC):
            units += slab_units(g, c * N) + slab_units(u, c * N)
            if c:
                units += row_units(d, (c - 1) * 4, 4)
        half = [(4, N, (lambda j=j: k_rows(g)[:, 4 * j:4 * j + 4, DC * N:FD],
                        lambda j=j: k_rows(u)[:, 4 * j:4 * j + 4, DC * N:FD])) for j in range(2)]
        return units + half + row_units(d, (DC - 1) * 4, 4) + row_units(d, DC * 4, 2)

    MIXER = 2 * 7 + 1 + 2 + 4
    STREAM = mixer_units(0) + dense_units() + mixer_units(1)
    U0 = len(STREAM)
    UI = FC * 6
    assert U0 == 2 * MIXER + 33 and U0 % SPLIT == 0 and UI % SPLIT == 0 and UI % RAW == 0

    def item_units(e):
        one = lambda w: w[0, bass.ds(e, 1)].rearrange("a r n -> (a r) n")
        g, u, d = one(moe_w_gate), one(moe_w_up), one(moe_w_down)
        units = []
        for c in range(FC):
            units += slab_units(g, c * N) + slab_units(u, c * N)
            if c:
                units += row_units(d, (c - 1) * 4, 4)
        return units + row_units(d, (FC - 1) * 4, 4)

    unit_width = lambda n: UNIT if n >= U0 else STREAM[n][0] * STREAM[n][1]

    PER_ITEM = dict(hi_ready=UI, lo_ready=UI, unit_used=UI, silu_ready=FC, act_ready=FC,
                    actT_landed=FC, actT_hi=FC, actT_ready=FC, y_hi_ready=2, y_ready=2, onehot_ready=1,
                    spreadT_landed=1, spreadT_ready=1, scatter_done=4, scatter_added=4, gather_done=2, rows_ready=2,
                    tokT_landed=2, tokT_hi_ready=KD, tokT_ready=KD)
    PLACES = RAW + 3
    OFTEN = {p: turn for turn, first in ((0, 0), (4, 4)) for p in (first, first + 9, first + 17, first + 25, first + 34)}
    ring_order = [(U0 + j) % RAW for j in range(RAW)] + list(range(RAW, PLACES))
    seldom = [place for turn, place in enumerate(ring_order) if turn not in (0, 4)]
    rest = [j for j in range(UI) if j not in OFTEN]
    assert len(rest) % len(seldom) == 0
    item_place = [ring_order[OFTEN[j]] if j in OFTEN else seldom[rest.index(j) % len(seldom)] for j in range(UI)]
    place_of, landed_at, unit_before, so_far, last_in = [], [], [], [0] * PLACES, [None] * PLACES
    for n in range(U0 + 2 * UI):
        slot = n % RAW if n < U0 else item_place[(n - U0) % UI]
        so_far[slot] += 32 if n < U0 and isinstance(STREAM[n][2], tuple) else 16
        place_of.append(slot)
        landed_at.append(so_far[slot])
        unit_before.append(last_in[slot])
        last_in[slot] = n
    for slot in range(PLACES):
        PER_ITEM[f"raw_landed{slot}"] = 16 * item_place.count(slot)

    def where(n, in_loop):
        if not in_loop:
            return place_of[n], landed_at[n], unit_before[n]
        return place_of[n], landed_at[n], unit_before[n + UI] - UI

    with ExitStack() as ctx:
        def sb(name, shape, dt=F32):
            return ctx.enter_context(nc.sbuf_tensor(name, shape, dt))

        def sem(name):
            return ctx.enter_context(nc.semaphore(name))

        raw = sb("raw", [P, RAW, UNIT])
        w_hi = sb("w_hi", [P, SPLIT, UNIT], F32R)
        w_lo = sb("w_lo", [P, SPLIT, UNIT], F32R)
        xs = sb("xs", [P, TB, D])
        work = sb("work", [P, TB, D])
        hT_hi = sb("hT_hi", [P, KD, S], F32R)
        hT_lo = sb("hT_lo", [P, KD, S], F32R)
        tokA = sb("tokA", [P, TB, N])
        tokP = sb("tokP", [P, TB, N])
        mix = sb("mix", [P, CC * (PAD + S) + GROUPS * (2 * P + REACH)])
        u_end, b_end = CC * (PAD + S), CC * (PAD + S) + GROUPS * (P + REACH)
        uT = mix[:, 0:u_end].rearrange("p (c t) -> p c t", c=CC)
        band_0 = mix[:, u_end:b_end].rearrange("p (g t) -> p g t", g=GROUPS)
        band_1 = mix[:, b_end:].rearrange("p (g t) -> p g t", g=GROUPS)
        tap_prod = sb("tap_prod", [P, PRODS, S])
        conv = work[:, 0, :].rearrange("p (c t) -> p c t", c=CC)
        gates = sb("gates", [P, TB, 2, D])
        gate_c = gates[:, :, 0, :]
        gate_p = gates[:, :, 1, :]
        onehot, spreadT = sb("onehot", [P, TB, P], F32R), sb("spreadT", [P, TB, P], F32R)
        y_hi, y_lo = sb("y_hi", [P, D], F32R), sb("y_lo", [P, D], F32R)
        cT_hi = sb("cT_hi", [P, CC * S], F32R)
        cT_lo = sb("cT_lo", [P, CC * S], F32R)
        dT_hi = sb("dT_hi", [P, GROUPS * S], F32R)
        dT_lo = sb("dT_lo", [P, GROUPS * S], F32R)
        row_gain = sb("row_gain", [P, D])
        ident = sb("ident", [P, P])
        mean_w = sb("mean_w", [P, P])
        vecs = sb("vecs", [P, 56])
        taps = sb("taps", [P, 2, 124])
        small = sb("small", [P, 16])
        rw = sb("rw", [P, KD, E])
        carved = [0]

        def carve(*shape):
            n = int(np.prod(shape))
            flat = tap_prod[:, :, :].rearrange("p a b -> p (a b)")[:, carved[0]:carved[0] + n]
            carved[0] += n
            names = "abc"[:len(shape)]
            return flat.rearrange(f"p ({' '.join(names)}) -> p {' '.join(names)}", **dict(zip(names, shape)))

        ones = carve(P)
        before = carve(P)
        slot_no = carve(P)
        slot_int = carve(P).bitcast(I32)
        logT = carve(S)[0:E, :]
        route = carve(8, TB, E)
        rev = carve(TB, E)
        expert = carve(E)
        earlier = carve(E, E)
        over = carve(2, E)
        over_sum = carve(E, E)
        over_sel = carve(OVER, E)
        over_idx = carve(OVER, E)
        over_part = carve(OVER, TB, E)
        over_val = carve(4, OVER)
        over_col = carve(OVER, TB)
        pair = carve(8, TB)
        slot_of = sb("slot_of", [P, TABLE * TB])
        comb_of = sb("comb_of", [P, TABLE * TB])
        items = sb("items", [P, 8], I32)
        vec_rows = work[:, 0, 0:P]
        tap_rows = work[:, 0, P:3 * P].rearrange("p (l c) -> p l c", l=L)
        sq = work[:, 1, :]
        diag = gates[:, 1, :, :].rearrange("p a (i t) -> p (a i) t", t=P)
        junk, tok_rows = gate_c[:, 0, :], gate_p[:, 0, :]
        xn_hi, xn_lo = (t[:, :, :].rearrange("p (b k) s -> p b (k s)", b=TB) for t in (hT_hi, hT_lo))
        hT = work[:, :, :].rearrange("p b (k s) -> p (b k) s", s=S)
        ln_std, ln_rstd = sq[:, 0:S], sq[:, S:2 * S]
        act_hi = cT_hi[:, :].rearrange("p (b f t) -> p b f t", b=TB, f=4)
        act_lo = cT_lo[:, :].rearrange("p (b f t) -> p b f t", b=TB, f=4)
        tokT_hi = dT_hi[:, :].rearrange("p (k t) -> p k t", k=KD)
        tokT_lo = dT_lo[:, :].rearrange("p (k t) -> p k t", k=KD)
        place = [raw[:, i, :] for i in range(RAW)]
        place += [mix[:, 0:UNIT], gates[:, 1, :, :].rearrange("p a d -> p (a d)"), work[:, :, :].rearrange("p b d -> p (b d)")]
        bank = [ctx.enter_context(nc.psum_tensor(f"bank{i}", [P, N], F32)) for i in range(8)]

        raw_landed = [sem(f"raw_landed{i}") for i in range(PLACES)]
        hi_ready, lo_ready, unit_used = sem("hi_ready"), sem("lo_ready"), sem("unit_used")
        x_landed = [sem(f"x_landed{h}") for h in range(2)]
        vecs_landed, taps_landed, rw_landed = sem("vecs_landed"), sem("taps_landed"), sem("rw_landed")
        gain_landed, consts_ready, pool_step = sem("gain_landed"), sem("consts_ready"), sem("pool_step")
        vecT_done, vecs_ready = sem("vecT_done"), sem("vecs_ready")
        tapsT_done, taps_ready = sem("tapsT_done"), sem("taps_ready")
        result_ready, out_stored = sem("result_ready"), sem("out_stored")
        sumsq_ready, meansq_ready, rstd_ready = sem("sumsq_ready"), sem("meansq_ready"), sem("rstd_ready")
        xn_ready, xT_done, hT_hi_ready, hT_ready = sem("xn_ready"), sem("xT_done"), sem("hT_hi_ready"), sem("hT_ready")
        x_ready, dve_step = sem("x_ready"), sem("dve_step")
        left_done = sem("left_done")
        sig_ready, u_ready, p_ready = sem("sig_ready"), sem("u_ready"), sem("p_ready")
        gates_ready, gate_p_scaled = sem("gates_ready"), sem("gate_p_scaled")
        uT_done, uT_ready, conv_step = sem("uT_done"), sem("uT_ready"), sem("conv_step")
        prod_ready, prod_added, diag_ready, pe_taps_done = sem("prod_ready"), sem("prod_added"), sem("diag_ready"), sem("pe_taps_done")
        pooled_done, dT_hi_ready, dT_ready = sem("pooled_done"), sem("dT_hi_ready"), sem("dT_ready")
        mean_done, centred, centred_sq, var_done = sem("mean_done"), sem("centred"), sem("centred_sq"), sem("var_done")
        std_ready, normed, sig_conv, silu_conv = sem("std_ready"), sem("normed"), sem("sig_conv"), sem("silu_conv")
        cT_hi_ready, cT_ready = sem("cT_hi_ready"), sem("cT_ready")
        yp_merged, yc_gated, merged_ready = sem("yp_merged"), sem("yc_gated"), sem("merged_ready")
        silu_ready, act_ready = sem("silu_ready"), sem("act_ready")
        actT_landed, actT_hi, actT_ready = sem("actT_landed"), sem("actT_hi"), sem("actT_ready")
        y_hi_ready, y_ready = sem("y_hi_ready"), sem("y_ready")
        routerT_act, routerT_dve, logitsT_done, logT_ready = sem("routerT_act"), sem("routerT_dve"), sem("logitsT_done"), sem("logT_ready")
        logits_done, diff_ready, probs_ready = sem("logits_done"), sem("diff_ready"), sem("probs_ready")
        mask_ready, rank_done, total_done, tables_ready = sem("mask_ready"), sem("rank_done"), sem("total_done"), sem("tables_ready")
        xn_hi_ready = sem("xn_hi_ready")
        onehot_ready, gather_done, rows_ready = sem("onehot_ready"), sem("gather_done"), sem("rows_ready")
        tokT_landed, tokT_hi_ready, tokT_ready = sem("tokT_landed"), sem("tokT_hi_ready"), sem("tokT_ready")
        spreadT_landed, spreadT_ready = sem("spreadT_landed"), sem("spreadT_ready")
        scatter_done, scatter_added = sem("scatter_done"), sem("scatter_added")

        X_BANKS, MERGED_BANKS = (4, 6, 5, 7), (0, 2, 1, 3)
        V_MIX, V_FFN, V_CB, V_LG, V_LB = 0, 16, 32, 40, 48

        block = ctx.enter_context(nc.Block())


        @block.sync
        def _(sp):
            seen = Seen(PER_ITEM)

            def load(n, unit):
                blocks, width, source = unit
                slot, _, before = where(n, seen.item is not None)
                if before is not None:
                    sp.wait_ge(lo_ready, seen.at(lo_ready, before + 1))
                elif slot == RAW + 2:
                    sp.wait_ge(logitsT_done, 1)
                elif slot >= RAW:
                    sp.wait_ge(unit_used, U0 - 3)
                dst = place[slot][:, 0:blocks * width].rearrange("p (k n) -> p k n", k=blocks)
                if isinstance(source, tuple):
                    half = width // 2
                    sp.dma_start(dst[:, :, 0:half], source[0]()).then_inc(raw_landed[slot], 16)
                    sp.dma_start(dst[:, :, half:], source[1]()).then_inc(raw_landed[slot], 16)
                else:
                    sp.dma_start(dst, source()).then_inc(raw_landed[slot], 16)

            def load_x(h):
                half = slice(h * N, (h + 1) * N)
                sp.dma_start(xs[:, :, half], x[0].rearrange("(b p) d -> p b d", p=P)[:, :, half]).then_inc(x_landed[h], 16)

            rows = 0
            for v, per in ((mix_norm, KD), (ffn_norm, KD), (conv_dw_b, CC), (conv_ln_g, CC), (conv_ln_b, CC)):
                sp.dma_start(vec_rows[rows:rows + L * per, :], v.rearrange("l (k p) -> (l k) p", p=P)).then_inc(vecs_landed, 16)
                rows += L * per
            load_x(0)
            load(0, STREAM[0])
            for l in range(L):
                sp.dma_start(tap_rows[0:TAPS * CC, l, :], conv_dw[l].rearrange("j (c p) -> (j c) p", p=P)).then_inc(taps_landed, 16)
            load_x(1)
            for n, unit in enumerate(STREAM[1:], 1):
                load(n, unit)
            for j, unit in enumerate(item_units(0)):
                load(U0 + j, unit)
            with sp.Fori(1, E) as i:
                seen.item = i
                for j, unit in enumerate(item_units(i)):
                    load(U0 + j, unit)
            seen.item = None
            sp.wait_ge(tables_ready, 1)
            n_items = sp.value_load(items[0:1, 0:1], min_val=E, max_val=E + OVER)
            with sp.If(n_items > E):
                with sp.Fori(E, n_items) as i:
                    seen.item = i
                    e = sp.value_load(items[0:1, bass.ds(i - (E - 1), 1)], min_val=0, max_val=E - 1)
                    for j, unit in enumerate(item_units(e)):
                        load(U0 + j, unit)
            for b in range(TB):
                sp.wait_ge(result_ready, b + 1)
                sp.dma_start(out[0, b * P:(b + 1) * P, :], xs[:, b, :]).then_inc(out_stored, 16)
            sp.wait_ge(out_stored, 16 * TB)

        @block.gpsimd
        def _(pool):
            seen = Seen(PER_ITEM)
            steps = [0]

            def step(ins):
                steps[0] += 1
                ins.then_inc(pool_step, 1)
                pool.wait_ge(pool_step, steps[0])

            step(pool.memset(ident[:, :], 0.0))
            step(pool.affine_select(out=ident[:, :], in_=ident[:, :], compare_op=ALU.not_equal, fill=1.0, base=0,
                                    pattern=[[-1, P]], channel_multiplier=1))
            pool.memset(small[:, 4:6], -0.5)
            pool.memset(small[:, 13:14], LN_EPS)
            pool.memset(uT[:, :, 0:PAD], 0.0)
            step(pool.memset(mean_w[:, :], 1.0 / CD))
            pool.memset(small[:, 12:13], 0.0).then_inc(consts_ready, 1)

            def inverse_root():
                pool.wait_ge(meansq_ready, seen.next(meansq_ready))
                pool.tensor_tensor(small[:, 6:8], small[:, 2:4], small[:, 4:6], ALU.pow).then_inc(rstd_ready, 1)

            def tap_diagonals(l):
                for j in range(TP):
                    ins = pool.tensor_scalar(diag[:, j, :], ident[:, :], taps[:, l, CC * j + 2:CC * j + 3], None, ALU.mult)
                ins.then_inc(diag_ready, 1)

            pool.wait_ge(taps_ready, L)
            tap_diagonals(0)
            inverse_root()
            for g, w in enumerate(WINDOWS):
                pool.memset(band_0[:, g, w - 1:], 1.0 / w)
                for t in range(w - 1):
                    pool.memset(band_0[:, g, t:t + 1], 1.0 / (t + 1))
                step(pool.memset(band_1[:, g, :], 1.0 / w))
                for band, cols in ((band_0, P + REACH), (band_1, P)):
                    step(pool.affine_select(out=band[:, g, :], in_=band[:, g, :], compare_op=ALU.is_ge, fill=0.0, base=0,
                                            pattern=[[1, cols]], channel_multiplier=-1))
                    step(pool.affine_select(out=band[:, g, :], in_=band[:, g, :], compare_op=ALU.is_ge, fill=0.0,
                                            base=w - 1, pattern=[[-1, cols]], channel_multiplier=1))
                    step(pool.tensor_tensor(band[:, g, 0:P], band[:, g, 0:P], ident[:, :], ALU.subtract))
            pool.memset(small[:, 12:13], 0.0).then_inc(consts_ready, 1)

            def router_constants():
                step(pool.memset(ones[:, :], 1.0))
                step(pool.affine_select(out=before[:, :], in_=ones[:, :], compare_op=ALU.is_gt, fill=0.0, base=0,
                                        pattern=[[1, P]], channel_multiplier=-1))
                step(pool.iota(slot_int[:, :], pattern=[[1, P]], base=0, channel_multiplier=0))
                step(pool.tensor_copy(slot_no[:, :], slot_int[:, :]))
                for e in range(E):
                    pool.memset(rev[:, :, e:e + 1], float(E - e))
                    pool.memset(expert[:, e:e + 1], float(e))
                    if e:
                        pool.memset(earlier[:, e, 0:e], 1.0)
                    pool.memset(earlier[:, e, e:E], 0.0)
                pool.memset(slot_of[:, :], NOWHERE)
                step(pool.memset(comb_of[:, :], 0.0))
                pool.memset(small[:, 12:13], 0.0).then_inc(consts_ready, 1)

            for l in range(L):
                for c, first, n, before_this in ADDS:
                    pool.wait_ge(prod_ready, len(PRODUCTS) * l + n + 1)
                    if before_this:
                        pool.wait_ge(prod_added, len(ADDS) * l + before_this)
                    part = conv[:, c, :] if first is None else tap_prod[:, (len(PRODUCTS) * l + first) % PRODS, :]
                    pool.tensor_tensor(conv[:, c, :], part, tap_prod[:, (len(PRODUCTS) * l + n) % PRODS, :],
                                       ALU.add).then_inc(prod_added, 1)
                pool.wait_ge(gain_landed, seen.next(gain_landed, 16))
                pool.wait_ge(gates_ready, seen.next(gates_ready, 2 * TB))
                for h in range(2):
                    for b in range(TB):
                        pool.wait_ge(gates_ready, seen.next(gates_ready))
                        part = gate_p[:, b, h * N:(h + 1) * N]
                        pool.tensor_tensor(part, part, row_gain[:, h * N:(h + 1) * N], ALU.mult).then_inc(gate_p_scaled, 1)
                if l == L - 1:
                    router_constants()
                inverse_root()
                if l == 0:
                    tap_diagonals(1)
                    inverse_root()
            for b in range(TB):
                pool.wait_ge(meansq_ready, seen.next(meansq_ready))
                pool.tensor_tensor(small[:, 6 + b:7 + b], small[:, 2 + b:3 + b], small[:, 4 + b:5 + b],
                                   ALU.pow).then_inc(rstd_ready, 1)

        def run_items(eng, seen, unit, item):
            base = dict(seen.n)
            item(0)
            for name, n in seen.n.items():
                assert n - base.get(name, 0) in (0, PER_ITEM.get(name, 0)), name

            def loop_body(i):
                seen.n = dict(base)
                seen.item, unit[0] = i, U0
                item(i)

            with eng.Fori(1, E) as i:
                loop_body(i)
            seen.item = None
            eng.wait_ge(tables_ready, 1)
            n_items = eng.value_load(items[0:1, 0:1], min_val=E, max_val=E + OVER)
            with eng.If(n_items > E):
                with eng.Fori(E, n_items) as i:
                    loop_body(i)
            seen.n, seen.item = dict(base), n_items
            return n_items

        @block.scalar
        def _(act):
            seen = Seen(PER_ITEM)
            unit = [0]

            def split_to(n):
                while unit[0] < n:
                    u = unit[0]
                    slot, landed, _ = where(u, seen.item is not None)
                    act.wait_ge(raw_landed[slot], seen.at(raw_landed[slot], landed))
                    if u >= SPLIT:
                        act.wait_ge(unit_used, seen.at(unit_used, u - SPLIT + 1))
                    width = unit_width(u)
                    act.activation(w_hi[:, u % SPLIT, 0:width], place[slot][:, 0:width], ACT.Copy).then_inc(hi_ready, 1)
                    unit[0] += 1

            def rstd(b):
                return small[:, 6 + b:7 + b]

            def sums_of_squares():
                for b in range(TB):
                    act.activation(junk, xs[:, b, :], ACT.Square, accum_out=small[:, b:b + 1]).then_inc(sumsq_ready, 1)
                    act.wait_ge(sumsq_ready, seen.next(sumsq_ready))

            def operand(gain, banks):
                for k in range(KD):
                    if k % 2 == 0:
                        act.wait_ge(xT_done, seen.next(xT_done))
                    scale = 1.0 if gain is None else vecs[:, gain + k:gain + k + 1]
                    act.activation(hT_hi[:, k, :], bank[banks[k // 2]][:, (k % 2) * S:(k % 2 + 1) * S], ACT.Copy,
                                   scale=scale).then_inc(hT_hi_ready, 1)

            prods = [0]

            def tap_products(l, n):
                while prods[0] < len(PRODUCTS) * l + n:
                    c, j = PRODUCTS[prods[0] - len(PRODUCTS) * l]
                    if prods[0] >= PRODS:
                        old_l, old = divmod(prods[0] - PRODS, len(PRODUCTS))
                        act.wait_ge(prod_added, len(ADDS) * old_l + PRODUCT_USED[old])
                    tap = taps[:, l, CC * j + c:CC * j + c + 1]
                    bias = vecs[:, V_CB + CC * l + c:V_CB + CC * l + c + 1] if j == 0 else 0.0
                    act.activation(tap_prod[:, prods[0] % PRODS, :], uT[:, c, j:j + S], ACT.Identity, scale=tap,
                                   bias=bias).then_inc(prod_ready, 1)
                    prods[0] += 1

            def gate_half(U, s):
                dst, c = (gate_c, gate_p)[s // 2], (s % 2) * N
                act.wait_ge(unit_used, seen.at(unit_used, U + 8 + 2 * s))
                for b in range(TB):
                    act.activation(dst[:, b, c:c + N], bank[2 * ((s + 1) % 2) + b][:, :], ACT.Sigmoid,
                                   scale=rstd(b)).then_inc(gates_ready, 1)

            def mixer(l, U):
                split_to(U + 2 if l else 1)
                operand(V_MIX + KD * l, X_BANKS)
                if l == 0:
                    for i in range(L):
                        act.wait_ge(tapsT_done, i + 1)
                        act.activation(taps[:, i, :], bank[2 + i][:, 0:TAPS * CC], ACT.Copy).then_inc(taps_ready, 1)
                    act.wait_ge(taps_ready, L)
                split_to(U + 3)
                if l:
                    act.wait_ge(x_ready, seen.next(x_ready, 2 * TB))
                else:
                    for h in range(2):
                        act.wait_ge(x_landed[h], 16)
                sums_of_squares()
                split_to(U + 5)
                act.wait_ge(unit_used, seen.at(unit_used, U + 2))
                act.wait_ge(rstd_ready, seen.next(rstd_ready))
                for b in range(TB):
                    act.activation(tokA[:, b, :], bank[b][:, :], ACT.Sigmoid, scale=rstd(b)).then_inc(sig_ready, 1)
                split_to(U + 8)
                for j in range(2):
                    act.wait_ge(uT_done, seen.next(uT_done))
                    act.activation(uT[:, 2 * j:2 * j + 2, PAD:], bank[6 + j][:, :].rearrange("p (c t) -> p c t", c=2),
                                   ACT.Copy).then_inc(uT_ready, 1)
                act.wait_ge(uT_ready, seen.next(uT_ready, 2))
                tap_products(l, 6)
                if l == 0:
                    act.dma_start(row_gain[:, :], pool_scale[0:1, :].to_broadcast([P, D])).then_inc(gain_landed, 16)
                    act.dma_start(rw[:, :, :], router_w[0].rearrange("(k p) e -> p k e", p=P)).then_inc(rw_landed, 16)
                split_to(U + 9)
                act.wait_ge(unit_used, seen.at(unit_used, U + 6))
                for b in range(TB):
                    act.activation(tokP[:, b, :], bank[b][:, :], ACT.Copy, scale=rstd(b)).then_inc(p_ready, 1)
                for s in range(3):
                    tap_products(l, 12 + 14 * s)
                    split_to(U + 10 + 2 * s)
                    if s == 1:
                        for j in range(2):
                            act.wait_ge(pooled_done, seen.next(pooled_done))
                            act.activation(dT_hi[:, 2 * j * S:2 * (j + 1) * S], bank[6 + j][:, :], ACT.Copy).then_inc(dT_hi_ready, 1)
                    tap_products(l, (19, 33, len(PRODUCTS))[s])
                    if s < 2:
                        split_to(U + 11 + 2 * s)
                    gate_half(U, s)
                act.wait_ge(centred, seen.next(centred))
                act.activation(sq, work[:, 0, :], ACT.Square).then_inc(centred_sq, 1)
                split_to(U + 15)
                act.wait_ge(var_done, seen.next(var_done))
                act.activation(ln_std[:, :], bank[7][:, 0:S], ACT.Sqrt, bias=small[:, 13:14]).then_inc(std_ready, 1)
                split_to(U + 16)
                act.wait_ge(normed, seen.next(normed))
                for c in range(CC):
                    g, b = (vecs[:, v:v + 1] for v in (V_LG + CC * l + c, V_LB + CC * l + c))
                    act.activation(sq[:, c * S:(c + 1) * S], conv[:, c, :], ACT.Sigmoid, bias=b, scale=g)
                    act.activation(conv[:, c, :], conv[:, c, :], ACT.Identity, bias=b, scale=g).then_inc(sig_conv, 1)
                gate_half(U, 3)
                for c in range(CC):
                    act.wait_ge(silu_conv, seen.next(silu_conv))
                    act.activation(cT_hi[:, c * S:(c + 1) * S], conv[:, c, :], ACT.Copy).then_inc(cT_hi_ready, 1)
                split_to(U + 19)
                operand(None, MERGED_BANKS)
                split_to(U + 21)
                act.wait_ge(gate_p_scaled, 2 * TB * (l + 1))
                row = pool_scale[l + 1:l + 2, :] if l + 1 < L else final_norm.rearrange("(a d) -> a d", a=1)
                act.dma_start(row_gain[:, :], row.to_broadcast([P, D])).then_inc(gain_landed, 16)

            def silu_of_gate(c, g, width):
                act.wait_ge(unit_used, seen.at(unit_used, g + 2))
                for b in range(TB):
                    if c:
                        act.wait_ge(act_ready, seen.at(act_ready, TB * (c - 1) + b + 1))
                    act.activation(tokA[:, b, 0:width], bank[b][:, 0:width], ACT.Silu, scale=rstd(b)).then_inc(silu_ready, 1)

            def hidden_hi(n):
                for b in range(TB):
                    act.wait_ge(actT_landed, seen.next(actT_landed))
                    act.activation(act_hi[:, b, 0:n, :], bank[2 + b][:, 0:n * P].rearrange("p (f t) -> p f t", f=n),
                                   ACT.Copy).then_inc(actT_hi, 1)

            act.wait_ge(vecT_done, 1)
            act.activation(vecs[:, :], bank[0][:, 0:56], ACT.Copy).then_inc(vecs_ready, 1)
            act.wait_ge(vecs_ready, 1)
            act.wait_ge(consts_ready, 1)
            mixer(0, 0)

            U = MIXER
            split_to(U + 2)
            operand(V_FFN, X_BANKS)
            split_to(U + 3)
            act.wait_ge(x_ready, seen.next(x_ready, 2 * TB))
            sums_of_squares()
            act.wait_ge(rstd_ready, seen.next(rstd_ready))
            for c in range(DC + 1):
                g = U + max(0, 6 * c - 2)
                split_to(g + 4)
                if c:
                    hidden_hi(4)
                split_to(g + 5)
                silu_of_gate(c, g, N if c < DC else N // 2)
            hidden_hi(2)

            mixer(1, MIXER + 33)

            split_to(U0 + 2)
            for k in (0, 1, 4, 5):
                if k % 2 == 0:
                    act.wait_ge(xT_done, seen.next(xT_done, 1 if k == 0 else 2))
                g = V_FFN + KD + k
                act.activation(hT[:, k, :], bank[X_BANKS[k // 2]][:, (k % 2) * S:(k % 2 + 1) * S], ACT.Copy,
                               scale=vecs[:, g:g + 1]).then_inc(routerT_act, 1)
            act.wait_ge(x_ready, seen.next(x_ready, 2 * TB))
            sums_of_squares()
            act.wait_ge(logitsT_done, 1)
            act.activation(logT[:, :], bank[0][0:E, 0:S], ACT.Copy).then_inc(logT_ready, 1)
            act.wait_ge(rstd_ready, seen.next(rstd_ready))
            for b in range(TB):
                act.activation(xn_hi[:, b, :], xs[:, b, :], ACT.Copy, scale=rstd(b)).then_inc(xn_hi_ready, 1)

            def gathered_rows():
                for h in range(2):
                    act.wait_ge(gather_done, seen.next(gather_done))
                    act.activation(tok_rows[:, h * N:(h + 1) * N], bank[6 + h][:, :], ACT.Copy).then_inc(rows_ready, 1)

            def gathered_hi():
                for k in range(KD):
                    if k % 4 == 0:
                        act.wait_ge(tokT_landed, seen.next(tokT_landed))
                    g = V_FFN + KD + k
                    act.activation(tokT_hi[:, k, :], bank[6 + k // 4][:, (k % 4) * P:(k % 4 + 1) * P], ACT.Copy,
                                   scale=vecs[:, g:g + 1]).then_inc(tokT_hi_ready, 1)

            def result_of_item():
                act.wait_ge(unit_used, seen.at(unit_used, U0))
                for h in range(2):
                    act.activation(y_hi[:, h * N:(h + 1) * N], bank[4 + h][:, :], ACT.Copy).then_inc(y_hi_ready, 1)

            def scatter_matrix():
                act.wait_ge(spreadT_landed, seen.next(spreadT_landed))
                act.activation(spreadT[:, :, :], bank[3][:, 0:TB * P].rearrange("p (b t) -> p b t", b=TB),
                               ACT.Copy).then_inc(spreadT_ready, 1)

            def item_hidden_hi(slot=0):
                act.wait_ge(actT_landed, seen.next(actT_landed))
                act.activation(act_hi[:, slot, :, :], bank[2][:, :].rearrange("p (f t) -> p f t", f=4), ACT.Copy).then_inc(actT_hi, 1)

            act.wait_ge(diff_ready, seen.next(diff_ready))
            act.activation(pair[:, 4, :], pair[:, 3, :], ACT.Sigmoid).then_inc(probs_ready, 1)
            act.activation(pair[:, 5, :], pair[:, 3, :], ACT.Sigmoid, scale=-1.0).then_inc(probs_ready, 1)
            split_to(U0 + 3)
            seen.next(gather_done, 2)
            used_before = TB * (DC + 1)

            def item(i):
                split_to(U0 + 1)
                gathered_hi()
                split_to(U0 + 3)
                result_of_item()
                for c in range(FC):
                    g = U0 + max(0, 6 * c - 2)
                    split_to(g + 4)
                    if c:
                        item_hidden_hi()
                    if c == 3:
                        scatter_matrix()
                    if c == 5:
                        gathered_rows()
                    split_to(g + 5)
                    act.wait_ge(unit_used, seen.at(unit_used, g + 2))
                    act.wait_ge(act_ready, seen.at(act_ready, used_before + c))
                    act.activation(tokA[:, 0, :], bank[0][:, :], ACT.Silu).then_inc(silu_ready, 1)
                split_to(U0 + UI - 1)
                item_hidden_hi(1)
                split_to(U0 + UI)

            run_items(act, seen, unit, item)
            result_of_item()
            for b in range(TB):
                act.wait_ge(scatter_added, seen.at(scatter_added, 2 * (b + 1)))
                act.activation(junk, xs[:, b, :], ACT.Square, accum_out=small[:, b:b + 1]).then_inc(sumsq_ready, 1)
                act.wait_ge(sumsq_ready, seen.next(sumsq_ready))

        @block.vector
        def _(dve):
            seen = Seen(PER_ITEM)
            unit = [0]
            steps = [0]

            def step(ins):
                steps[0] += 1
                ins.then_inc(dve_step, 1)
                dve.wait_ge(dve_step, steps[0])

            def split_to(n):
                while unit[0] < n:
                    u = unit[0]
                    dve.wait_ge(hi_ready, seen.at(hi_ready, u + 1))
                    width = unit_width(u)
                    slot, _, _ = where(u, seen.item is not None)
                    dve.tensor_tensor(w_lo[:, u % SPLIT, 0:width], place[slot][:, 0:width],
                                      w_hi[:, u % SPLIT, 0:width].bitcast(F32), ALU.subtract).then_inc(lo_ready, 1)
                    unit[0] += 1

            def rstd(b):
                return small[:, 6 + b:7 + b]

            def mean_squares():
                dve.wait_ge(sumsq_ready, seen.next(sumsq_ready, TB))
                dve.tensor_scalar(small[:, 2:4], small[:, 0:2], 1.0 / D, RMS_EPS, ALU.mult, ALU.add).then_inc(meansq_ready, 1)

            def operand(gain, banks):
                for k in range(KD):
                    if k % 2 == 0:
                        dve.wait_ge(hT_hi_ready, seen.next(hT_hi_ready, 2))
                    src = bank[banks[k // 2]][:, (k % 2) * S:(k % 2 + 1) * S]
                    scale = 1.0 if gain is None else vecs[:, gain + k:gain + k + 1]
                    dve.scalar_tensor_tensor(hT_lo[:, k, :], src, scale, hT_hi[:, k, :].bitcast(F32),
                                             ALU.mult, ALU.subtract).then_inc(hT_ready, 1)

            conv_steps = [0]
            last_step = {}

            def conv_tap(l, j):
                for c in range(3 if TP <= j < TV else 2):
                    if c == 2 and j == TP:
                        dve.wait_ge(pe_taps_done, l + 1)
                    elif j:
                        dve.wait_ge(conv_step, last_step[c])
                    tap = taps[:, l, CC * j + c:CC * j + c + 1]
                    src = uT[:, c, j:j + S]
                    acc = bank[4 + c // 2][:, (c % 2) * S:(c % 2 + 1) * S]
                    if j == 0:
                        bias = vecs[:, V_CB + CC * l + c:V_CB + CC * l + c + 1]
                        ins = dve.tensor_scalar(acc, src, tap, bias, ALU.mult, ALU.add)
                    else:
                        dst = acc if j < TAPS - 1 else conv[:, c, :]
                        ins = dve.scalar_tensor_tensor(dst, src, tap, acc, ALU.mult, ALU.add)
                    ins.then_inc(conv_step, 1)
                    conv_steps[0] += 1
                    last_step[c] = conv_steps[0]

            def mixer(l, U):
                split_to(U + 2 if l else 1)
                operand(V_MIX + KD * l, X_BANKS)
                split_to(U + 3)
                mean_squares()
                split_to(U + 6)
                dve.wait_ge(unit_used, seen.at(unit_used, U + 4))
                dve.wait_ge(rstd_ready, seen.next(rstd_ready))
                for b in range(TB):
                    dve.wait_ge(sig_ready, seen.next(sig_ready))
                    dve.scalar_tensor_tensor(tokA[:, b, :], bank[2 + b][:, :], rstd(b), tokA[:, b, :], ALU.mult,
                                             ALU.mult).then_inc(u_ready, 1)
                split_to(U + 8)
                dve.wait_ge(uT_ready, seen.next(uT_ready, 2))
                dve.wait_ge(taps_ready, L)
                for j in range(TAPS):
                    if j >= 9 and (j - 9) % 4 == 0:
                        split_to(min(U + 9 + (j - 9) // 4, U + 14))
                    if j == 22:
                        for i in range(2):
                            dve.wait_ge(dT_hi_ready, seen.next(dT_hi_ready))
                            part = slice(2 * i * S, 2 * (i + 1) * S)
                            dve.tensor_tensor(dT_lo[:, part], bank[6 + i][:, :], dT_hi[:, part].bitcast(F32),
                                              ALU.subtract).then_inc(dT_ready, 1)
                    conv_tap(l, j)
                dve.wait_ge(conv_step, last_step[2])
                dve.wait_ge(prod_added, len(ADDS) * l + last_add[2])
                bias = vecs[:, V_CB + CC * l + 2:V_CB + CC * l + 3]
                dve.scalar_tensor_tensor(conv[:, 2, :], bank[5][:, 0:S], bias, conv[:, 2, :], ALU.add, ALU.add).then_inc(conv_step, 1)
                conv_steps[0] += 1
                split_to(U + 14)
                dve.wait_ge(mean_done, seen.next(mean_done))
                dve.tensor_tensor(conv[:, :, :], conv[:, :, :], bank[6][:, 0:S].unsqueeze(1).to_broadcast([P, CC, S]),
                                  ALU.subtract).then_inc(centred, 1)
                split_to(U + 15)
                dve.wait_ge(std_ready, seen.next(std_ready))
                step(dve.reciprocal(ln_rstd[:, :], ln_std[:, :]))
                dve.tensor_tensor(conv[:, :, :], conv[:, :, :], ln_rstd[:, :].unsqueeze(1).to_broadcast([P, CC, S]),
                                  ALU.mult).then_inc(normed, 1)
                split_to(U + 16)
                for c in range(CC):
                    dve.wait_ge(sig_conv, seen.next(sig_conv))
                    dve.tensor_tensor(conv[:, c, :], conv[:, c, :], sq[:, c * S:(c + 1) * S], ALU.mult).then_inc(silu_conv, 1)
                for c in range(CC):
                    dve.wait_ge(cT_hi_ready, seen.next(cT_hi_ready))
                    dve.tensor_tensor(cT_lo[:, c * S:(c + 1) * S], conv[:, c, :], cT_hi[:, c * S:(c + 1) * S].bitcast(F32),
                                      ALU.subtract).then_inc(cT_ready, 1)
                split_to(U + 17)
                dve.wait_ge(gate_p_scaled, seen.next(gate_p_scaled, 2 * TB))
                dve.wait_ge(unit_used, seen.at(unit_used, U + 15))
                for h in range(2):
                    for b in range(TB):
                        part = gate_p[:, b, h * N:(h + 1) * N]
                        dve.tensor_tensor(part, bank[2 * b + h][:, :], part, ALU.mult).then_inc(yp_merged, 1)
                split_to(U + 18)
                for h in range(2):
                    half_done(h, U + 17)
                    for b in range(TB):
                        part = gate_c[:, b, h * N:(h + 1) * N]
                        dve.tensor_tensor(part, bank[4 + 2 * b + h][:, :], part, ALU.mult).then_inc(yc_gated, 1)
                    if h == 0:
                        dve.wait_ge(yp_merged, seen.next(yp_merged, 2 * TB))
                    for b in range(TB):
                        part = slice(h * N, (h + 1) * N)
                        dve.wait_ge(yc_gated, seen.next(yc_gated))
                        dve.tensor_tensor(gate_c[:, b, part], gate_c[:, b, part], gate_p[:, b, part], ALU.add).then_inc(merged_ready, 1)
                operand(None, MERGED_BANKS)
                split_to(U + 23)
                add_to_x(U + 21)

            def half_done(h, units):
                if h == 0:
                    dve.wait_ge(left_done, seen.next(left_done))
                else:
                    dve.wait_ge(unit_used, seen.at(unit_used, units))

            def add_to_x(units):
                for h in range(2):
                    half_done(h, units)
                    for b in range(TB):
                        part = xs[:, b, h * N:(h + 1) * N]
                        dve.tensor_tensor(part, bank[4 + 2 * b + h][:, :], part, ALU.add).then_inc(x_ready, 1)

            def hidden_lo(n):
                for b in range(TB):
                    dve.wait_ge(actT_hi, seen.next(actT_hi))
                    dve.tensor_tensor(act_lo[:, b, 0:n, :], bank[2 + b][:, 0:n * P].rearrange("p (f t) -> p f t", f=n),
                                      act_hi[:, b, 0:n, :].bitcast(F32), ALU.subtract).then_inc(actT_ready, 1)

            dve.wait_ge(vecs_ready, 1)
            mixer(0, 0)

            U = MIXER
            operand(V_FFN, X_BANKS)
            split_to(U + 3)
            mean_squares()
            dve.wait_ge(rstd_ready, seen.next(rstd_ready))
            for c in range(DC + 1):
                g = U + max(0, 6 * c - 2)
                split_to(g + 4)
                if c:
                    hidden_lo(4)
                split_to(min(g + 7, U + 33))
                if c < DC:
                    dve.wait_ge(unit_used, seen.at(unit_used, g + 4))
                for b in range(TB):
                    dve.wait_ge(silu_ready, seen.next(silu_ready))
                    if c < DC:
                        up, width = bank[2 + b][:, :], N
                    else:
                        up, width = bank[b][:, N // 2:], N // 2
                    dve.scalar_tensor_tensor(tokP[:, b, 0:width], up, rstd(b), tokA[:, b, 0:width], ALU.mult,
                                             ALU.mult).then_inc(act_ready, 1)
            hidden_lo(2)
            split_to(U + 35)
            add_to_x(U + 33)

            mixer(1, MIXER + 33)

            for k in (2, 3, 6, 7):
                if k % 2 == 0:
                    dve.wait_ge(xT_done, (2 * L + 1) * KD // 2 + k // 2 + 1)
                g = V_FFN + KD + k
                dve.tensor_scalar(hT[:, k, :], bank[X_BANKS[k // 2]][:, (k % 2) * S:(k % 2 + 1) * S], vecs[:, g:g + 1], None,
                                  ALU.mult).then_inc(routerT_dve, 1)
            mean_squares()
            dve.wait_ge(consts_ready, 3)
            dve.memset(spreadT[:, :, :].bitcast(F32), 0.0)

            per_e = lambda v: v.unsqueeze(2).to_broadcast([P, TB, E])
            CAND, SEL1, LG2, SEL2, MASK, POS, T1, T2 = range(8)
            r = lambda i: route[:, i, :, :]
            LG = bank[1][:, 0:TB * E].rearrange("p (b e) -> p b e", b=TB)
            dve.wait_ge(logits_done, seen.next(logits_done))

            def best(values, v, sel):
                step(dve.tensor_reduce(pair[:, v, :], values, AX_X, ALU.max))
                for b in range(TB):
                    ins = dve.scalar_tensor_tensor(route[:, CAND, b, :], values[:, b, :], pair[:, v, b:b + 1], rev[:, b, :],
                                                   ALU.is_equal, ALU.mult)
                step(ins)
                step(dve.tensor_reduce(pair[:, 2, :], r(CAND), AX_X, ALU.max))
                step(dve.tensor_tensor(r(sel), rev[:, :, :], per_e(pair[:, 2, :]), ALU.is_equal))

            best(LG, 0, SEL1)
            step(dve.scalar_tensor_tensor(r(LG2), r(SEL1), -3.0e38, LG, ALU.mult, ALU.add))
            best(r(LG2), 1, SEL2)
            dve.tensor_tensor(r(MASK), r(SEL1), r(SEL2), ALU.add).then_inc(mask_ready, 1)

            def xn_rest(b):
                dve.wait_ge(xn_hi_ready, seen.next(xn_hi_ready))
                return dve.scalar_tensor_tensor(xn_lo[:, b, :], xs[:, b, :], rstd(b), xn_hi[:, b, :].bitcast(F32), ALU.mult,
                                                ALU.subtract)

            dve.wait_ge(rstd_ready, seen.next(rstd_ready))
            xn_rest(0)
            step(dve.tensor_tensor(pair[:, 2, :], pair[:, 0, :], pair[:, 1, :], ALU.subtract))
            dve.tensor_tensor(pair[:, 3, :], pair[:, 2, :], small[:, 6:8], ALU.mult).then_inc(diff_ready, 1)
            table = lambda t, i, n: t[:, i * TB:(i + n) * TB].rearrange("p (i b) -> p b i", b=TB)
            slots, combs = table(slot_of, 1, E), table(comb_of, 1, E)
            dve.wait_ge(rank_done, seen.next(rank_done))
            dve.wait_ge(mask_ready, 1)
            step(dve.scalar_tensor_tensor(r(POS), bank[3][:, 0:TB * E].rearrange("p (b e) -> p b e", b=TB), -NOWHERE,
                                          r(MASK), ALU.add, ALU.mult))
            step(dve.tensor_scalar(slots, r(POS), NOWHERE, None, ALU.add))

            def gather_matrix(column):
                for b in range(TB):
                    ins = dve.tensor_scalar(onehot[:, b, :], slot_no[:, :], slot_of[:, bass.ds(column * TB + b, 1)], None, ALU.is_equal)
                return ins

            gather_matrix(1)
            xn_rest(1).then_inc(onehot_ready, 1)

            N_OVER, HAS, SHIFT, INDEX = range(4)
            dve.wait_ge(total_done, 1)
            step(dve.tensor_scalar(over[:, 0, :], bank[2][:, 0:E], float(P), None, ALU.is_gt))
            step(dve.tensor_tensor(over_sum[:, :, :], earlier[:, :, :], over[:, 0, :].unsqueeze(1).to_broadcast([P, E, E]), ALU.mult))
            step(dve.tensor_reduce(over[:, 1, :], over_sum[:, :, :], AX_X, ALU.add))
            step(dve.tensor_reduce(over_val[:, N_OVER, 0:1], over[:, 0, :], AX_X, ALU.add))
            dve.tensor_scalar(items[:, 0:1], over_val[:, N_OVER, 0:1], float(E), None, ALU.add)
            for k in range(OVER):
                ins = dve.scalar_tensor_tensor(over_sel[:, k, :], over[:, 1, :], float(k), over[:, 0, :], ALU.is_equal, ALU.mult)
            step(ins)
            dve.tensor_tensor(over_idx[:, :, :], over_sel[:, :, :], expert[:, :].unsqueeze(1).to_broadcast([P, OVER, E]), ALU.mult)
            step(dve.tensor_reduce(over_val[:, HAS, :], over_sel[:, :, :], AX_X, ALU.add))
            step(dve.tensor_reduce(over_val[:, INDEX, :], over_idx[:, :, :], AX_X, ALU.add))
            dve.tensor_copy(items[:, 1:1 + OVER], over_val[:, INDEX, :])
            step(dve.tensor_scalar(over_val[:, SHIFT, :], over_val[:, HAS, :], -NOWHERE - P, NOWHERE, ALU.mult, ALU.add))

            def overflow_sums(values):
                for k in range(OVER):
                    ins = dve.tensor_tensor(over_part[:, k, :, :], values, over_sel[:, k, :].unsqueeze(1).to_broadcast([P, TB, E]), ALU.mult)
                step(ins)
                return over_part[:, :, :, :].rearrange("p k b e -> p (k b) e")

            over_columns = lambda t: t[:, (1 + E) * TB:(1 + E + OVER) * TB]
            step(dve.tensor_reduce(over_col[:, :, :].rearrange("p k b -> p (k b)"), overflow_sums(slots), AX_X, ALU.add))
            step(dve.tensor_tensor(over_columns(slot_of).rearrange("p (k b) -> p k b", b=TB), over_col[:, :, :],
                                   over_val[:, SHIFT, :].unsqueeze(2).to_broadcast([P, OVER, TB]), ALU.add))

            def combination_table():
                dve.wait_ge(probs_ready, seen.next(probs_ready, 2))
                dve.tensor_tensor(r(T1), r(SEL1), per_e(pair[:, 4, :]), ALU.mult)
                step(dve.tensor_tensor(r(T2), r(SEL2), per_e(pair[:, 5, :]), ALU.mult))
                step(dve.tensor_tensor(combs, r(T1), r(T2), ALU.add))
                dve.tensor_reduce(over_columns(comb_of), overflow_sums(combs), AX_X, ALU.add).then_inc(tables_ready, 1)

            def gathered_lo():
                for k in range(KD):
                    if k % 4 == 0:
                        dve.wait_ge(tokT_hi_ready, seen.next(tokT_hi_ready, 4))
                    g = V_FFN + KD + k
                    dve.scalar_tensor_tensor(tokT_lo[:, k, :], bank[6 + k // 4][:, (k % 4) * P:(k % 4 + 1) * P],
                                             vecs[:, g:g + 1], tokT_hi[:, k, :].bitcast(F32), ALU.mult,
                                             ALU.subtract).then_inc(tokT_ready, 1)

            def rest_of_result():
                for h in range(2):
                    part = slice(h * N, (h + 1) * N)
                    dve.wait_ge(y_hi_ready, seen.next(y_hi_ready))
                    dve.tensor_tensor(y_lo[:, part], bank[4 + h][:, :], y_hi[:, part].bitcast(F32), ALU.subtract).then_inc(y_ready, 1)

            def add_scattered(b, column, banks):
                for h in range(2):
                    dve.wait_ge(scatter_done, seen.next(scatter_done))
                    part = xs[:, b, h * N:(h + 1) * N]
                    dve.scalar_tensor_tensor(part, bank[banks[h]][:, :], comb_of[:, bass.ds(column * TB + b, 1)], part,
                                             ALU.mult, ALU.add).then_inc(scatter_added, 1)

            def item_hidden_lo(slot=0):
                dve.wait_ge(actT_hi, seen.next(actT_hi))
                dve.tensor_tensor(act_lo[:, slot, :, :], bank[2][:, :].rearrange("p (f t) -> p f t", f=4),
                                  act_hi[:, slot, :, :].bitcast(F32), ALU.subtract).then_inc(actT_ready, 1)

            combination_table()
            for h in range(2):
                dve.wait_ge(gather_done, h + 1)
                dve.tensor_copy(tok_rows[:, h * N:(h + 1) * N], bank[6 + h][:, :]).then_inc(rows_ready, 1)
            split_to(U0 + 3)

            def item(i):
                split_to(U0 + 1)
                gathered_lo()
                split_to(U0 + 3)
                rest_of_result()
                for c in range(FC):
                    g = U0 + max(0, 6 * c - 2)
                    split_to(g + 4)
                    if c:
                        item_hidden_lo()
                    if c == 2:
                        add_scattered(1, i, (6, 7))
                    if c == 3:
                        dve.wait_ge(spreadT_landed, seen.next(spreadT_landed))
                        gather_matrix(i + 2).then_inc(onehot_ready, 1)
                    split_to(g + (5 if c == 0 else 6 if c == FC - 1 else 7))
                    dve.wait_ge(silu_ready, seen.next(silu_ready))
                    dve.wait_ge(unit_used, seen.at(unit_used, g + 4))
                    dve.tensor_tensor(tokP[:, 0, :], bank[1][:, :], tokA[:, 0, :], ALU.mult).then_inc(act_ready, 1)
                    if c == 1:
                        add_scattered(0, i, (6, 7))
                split_to(U0 + UI - 1)
                item_hidden_lo(1)
                split_to(U0 + UI)

            n_items = run_items(dve, seen, unit, item)
            rest_of_result()
            add_scattered(0, n_items, (6, 7))
            add_scattered(1, n_items, (0, 1))
            seen.item = None
            dve.wait_ge(gain_landed, 16 * (L + 1))
            for b in range(TB):
                dve.wait_ge(sumsq_ready, seen.next(sumsq_ready))
                dve.tensor_scalar(small[:, 2 + b:3 + b], small[:, b:b + 1], 1.0 / D, RMS_EPS, ALU.mult, ALU.add).then_inc(meansq_ready, 1)
            for b in range(TB):
                dve.wait_ge(rstd_ready, seen.next(rstd_ready))
                dve.scalar_tensor_tensor(xs[:, b, :], xs[:, b, :], rstd(b), row_gain[:, :], ALU.mult,
                                         ALU.mult).then_inc(result_ready, 1)

        @block.tensor
        def _(pe):
            seen = Seen(PER_ITEM)

            def product(dst, a_hi, a_lo, b_hi, b_lo, start, stop):
                nc.tensor.matmul(dst, a_hi, b_hi, start=start, stop=False)
                nc.tensor.matmul(dst, a_hi, b_lo, start=False, stop=False)
                return nc.tensor.matmul(dst, a_lo, b_hi, start=False, stop=stop)

            def slab(U, a_hi, a_lo, banks, fresh=None, amid=None, between=None):
                for j in range(2):
                    pe.wait_ge(lo_ready, seen.at(lo_ready, U + j + 1))
                    s = (U + j) % SPLIT
                    for b, dst in enumerate(banks):
                        for kk in range(4):
                            k = 4 * j + kk
                            if fresh is not None and b == 0:
                                pe.wait_ge(fresh, seen.next(fresh))
                            last = product(dst, a_hi[:, k, b * P:(b + 1) * P], a_lo[:, k, b * P:(b + 1) * P],
                                           w_hi[:, s, kk * N:(kk + 1) * N], w_lo[:, s, kk * N:(kk + 1) * N],
                                           k == 0, k == KD - 1)
                        if (j, b) == (0, 0) and amid is not None:
                            amid()
                    last.then_inc(unit_used, 1)
                    if j == 0 and between is not None:
                        between()

            def rows(U, units, a_hi, a_lo, blocks, first_bank, start, stop, fresh=None, between=None, by_halves=False):
                for j in range(units):
                    pe.wait_ge(lo_ready, seen.at(lo_ready, U + j + 1))
                    s = (U + j) % SPLIT
                    steps = [(kk, b, h) for b in range(blocks) for kk in range(2) for h in range(2)]
                    if by_halves and j == units - 1:
                        steps = sorted(steps, key=lambda t: t[2])
                    for kk, b, h in steps:
                        if fresh is not None and b == 0 and h == 0:
                            pe.wait_ge(fresh, seen.next(fresh))
                        w = slice(kk * D + h * N, kk * D + (h + 1) * N)
                        last = product(bank[first_bank + 2 * b + h][:, :], a_hi(2 * j + kk, b), a_lo(2 * j + kk, b),
                                       w_hi[:, s, w], w_lo[:, s, w], start and j == 0 and kk == 0,
                                       stop and j == units - 1 and kk == 1)
                        if by_halves and j == units - 1 and (kk, b, h) == (1, blocks - 1, 0):
                            last.then_inc(left_done, 1)
                    last.then_inc(unit_used, 1)
                    if j == 0 and between is not None:
                        between()

            def transpose_x(source, banks, waits):
                for k in range(KD):
                    if k % 4 == 0:
                        waits(k // 4)
                    for b in range(TB):
                        last = nc.tensor.transpose(bank[banks[k // 2]][:, (k % 2) * S + b * P:(k % 2) * S + (b + 1) * P],
                                                   source[:, b, k * P:(k + 1) * P], ident[:, :])
                    if k % 2:
                        last.then_inc(xT_done, 1)

            def x_half(h):
                pe.wait_ge(x_ready, seen.next(x_ready, TB))

            def transpose_u():
                pe.wait_ge(u_ready, seen.next(u_ready, TB))
                for c in range(CC):
                    for b in range(TB):
                        last = nc.tensor.transpose(bank[6 + c // 2][:, (c % 2) * S + b * P:(c % 2) * S + (b + 1) * P],
                                                   tokA[:, b, c * P:(c + 1) * P], ident[:, :])
                    if c % 2:
                        last.then_inc(uT_done, 1)

            def pool_windows():
                pe.wait_ge(p_ready, seen.next(p_ready, TB))
                pe.wait_ge(consts_ready, 2)
                for g in range(GROUPS):
                    dst = bank[6 + g // 2][:, (g % 2) * S:(g % 2 + 1) * S]
                    first, second = (tokP[:, b, g * GD:(g + 1) * GD] for b in range(TB))
                    nc.tensor.matmul(dst[:, 0:P], first, band_0[:, g, 0:P], start=True, stop=True)
                    nc.tensor.matmul(dst[:, P:S], second, band_1[:, g, :], start=True, stop=False)
                    last = nc.tensor.matmul(dst[:, P:P + REACH], first, band_0[:, g, P:], start=False, stop=True)
                    if g % 2:
                        last.then_inc(pooled_done, 1)

            low, high = [bank[0][:, :], bank[1][:, :]], [bank[2][:, :], bank[3][:, :]]

            def mixer(l, U, x_waits):
                transpose_x(xs, X_BANKS, x_waits)
                if l == 0:
                    pe.wait_ge(taps_landed, 16 * L)
                    for i in range(L):
                        nc.tensor.transpose(bank[2 + i][:, 0:124], tap_rows[0:124, i, :], ident[0:124, 0:124]).then_inc(tapsT_done, 1)
                slab(U, hT_hi, hT_lo, low, fresh=hT_ready)
                pe.wait_ge(taps_ready, L)
                slab(U + 2, hT_hi, hT_lo, high)
                pe.wait_ge(sig_ready, seen.next(sig_ready, TB))
                slab(U + 4, hT_hi, hT_lo, low, between=transpose_u)
                pe.wait_ge(diag_ready, l + 1)
                pe.wait_ge(uT_ready, seen.next(uT_ready, 2))
                for j in range(TP):
                    last = nc.tensor.matmul(bank[5][:, 0:S], diag[:, j, :], uT[:, 2, j:j + S], start=j == 0, stop=j == TP - 1)
                last.then_inc(pe_taps_done, 1)
                slab(U + 6, hT_hi, hT_lo, high)
                pool_windows()
                slab(U + 8, hT_hi, hT_lo, low)
                pe.wait_ge(gates_ready, seen.next(gates_ready, TB))
                slab(U + 10, hT_hi, hT_lo, high)
                pe.wait_ge(dT_ready, seen.next(dT_ready, 2))
                for c in range(CC):
                    if c == CC - 1:
                        pe.wait_ge(prod_added, len(ADDS) * (l + 1))
                    else:
                        pe.wait_ge(conv_step, CONV_STEPS * (l + 1) - (c < 2))
                    last = nc.tensor.matmul(bank[6][:, 0:S], mean_w[:, :], conv[:, c, :], start=c == 0, stop=c == CC - 1)
                last.then_inc(mean_done, 1)

                def variance():
                    pe.wait_ge(centred_sq, seen.next(centred_sq))
                    for c in range(CC):
                        last = nc.tensor.matmul(bank[7][:, 0:S], mean_w[:, :], sq[:, c * S:(c + 1) * S], start=c == 0, stop=c == CC - 1)
                    last.then_inc(var_done, 1)

                pe.wait_ge(gates_ready, seen.next(gates_ready, TB))
                slab(U + 12, hT_hi, hT_lo, low, amid=variance)
                pe.wait_ge(lo_ready, seen.at(lo_ready, U + 15))
                s = (U + 14) % SPLIT
                for b in reversed(range(TB)):
                    pe.wait_ge(gates_ready, seen.next(gates_ready, TB))
                    for g in range(GROUPS):
                        a = slice(g * S + b * P, g * S + (b + 1) * P)
                        w = slice(g * GO, (g + 1) * GO)
                        last = product(bank[2 * b + g // 2][:, (g % 2) * GO:(g % 2 + 1) * GO], dT_hi[:, a], dT_lo[:, a],
                                       w_hi[:, s, w], w_lo[:, s, w], True, True)
                last.then_inc(unit_used, 1)
                cols = lambda t: (lambda k, b: t[:, k * S + b * P:k * S + (b + 1) * P])
                rows(U + 15, 2, cols(cT_hi), cols(cT_lo), TB, 4, True, True, fresh=cT_ready, by_halves=True)
                transpose_x(gate_c, MERGED_BANKS, merged)
                cols = lambda t: (lambda k, b: t[:, k, b * P:(b + 1) * P])
                rows(U + 17, 4, cols(hT_hi), cols(hT_lo), TB, 4, True, True, fresh=hT_ready, by_halves=True)

            def hidden_transposes(blocks, n, banks):
                for b in range(blocks):
                    pe.wait_ge(act_ready, seen.next(act_ready))
                    for f in range(n):
                        last = nc.tensor.transpose(bank[banks + b][:, f * P:(f + 1) * P], tokP[:, b, f * P:(f + 1) * P], ident[:, :])
                    last.then_inc(actT_landed, 1)

            hidden = lambda t: (lambda f, b: t[:, b, f, :])

            def merged(h):
                pe.wait_ge(merged_ready, seen.next(merged_ready, TB))

            def x_loaded(h):
                pe.wait_ge(x_landed[h], 16)

            pe.wait_ge(vecs_landed, 16 * 5)
            pe.wait_ge(consts_ready, 1)
            nc.tensor.transpose(bank[0][:, 0:56], vec_rows[0:56, :], ident[0:56, 0:56]).then_inc(vecT_done, 1)
            pe.wait_ge(vecs_ready, 1)
            mixer(0, 0, x_loaded)

            U = MIXER
            transpose_x(xs, X_BANKS, x_half)
            for c in range(DC + 1):
                g = U + max(0, 6 * c - 2)
                if c:
                    pe.wait_ge(silu_ready, seen.at(silu_ready, TB * c))
                slab(g, hT_hi, hT_lo, low, fresh=hT_ready if c == 0 else None,
                     between=(lambda: hidden_transposes(TB, 4, 2)) if c else None)
                if c < DC:
                    if c:
                        pe.wait_ge(actT_ready, seen.next(actT_ready, TB))
                    slab(g + 2, hT_hi, hT_lo, high)
                else:
                    pe.wait_ge(actT_ready, seen.next(actT_ready, TB))
                if c:
                    rows(g + (4 if c < DC else 2), 2, hidden(act_hi), hidden(act_lo), TB, 4, c == 1, False,
                         between=(lambda: hidden_transposes(TB, 2, 2)) if c == DC else None)
            pe.wait_ge(actT_ready, seen.next(actT_ready, TB))
            rows(U + 32, 1, hidden(act_hi), hidden(act_lo), TB, 4, False, True, by_halves=True)

            mixer(1, MIXER + 33, x_half)

            transpose_x(xs, X_BANKS, x_half)
            pe.wait_ge(rw_landed, 16)
            for k in range(KD):
                if k % 4 < 2:
                    pe.wait_ge(routerT_act, seen.next(routerT_act))
                else:
                    pe.wait_ge(routerT_dve, seen.next(routerT_dve))
                last = nc.tensor.matmul(bank[0][0:E, 0:S], rw[:, k, :], hT[:, k, :], start=k == 0, stop=k == KD - 1)
            last.then_inc(logitsT_done, 1)
            pe.wait_ge(logT_ready, 1)
            for b in range(TB):
                last = nc.tensor.transpose(bank[1][:, b * E:(b + 1) * E], logT[:, b * P:(b + 1) * P], ident[0:E, 0:E])
            last.then_inc(logits_done, 1)
            pe.wait_ge(consts_ready, 3)
            pe.wait_ge(mask_ready, seen.next(mask_ready))
            MASK = 4
            mask = route[:, MASK, :, :]
            nc.tensor.matmul(bank[3][:, 0:TB * E], before[:, :], mask.rearrange("p b e -> p (b e)"), start=True, stop=False)
            nc.tensor.matmul(bank[3][:, E:2 * E], ones[:, :], mask[:, 0, :], start=False, stop=True).then_inc(rank_done, 1)

            nc.tensor.matmul(bank[2][:, 0:E], ones[:, :], mask[:, 0, :], start=True, stop=False)
            nc.tensor.matmul(bank[2][:, 0:E], ones[:, :], mask[:, 1, :], start=False, stop=True).then_inc(total_done, 1)

            def gather():
                pe.wait_ge(onehot_ready, seen.next(onehot_ready))
                for h in range(2):
                    for b in range(TB):
                        for part in (xn_hi, xn_lo):
                            last = nc.tensor.matmul(bank[6 + h][:, :], onehot[:, b, :], part[:, b, h * N:(h + 1) * N],
                                                    start=b == 0 and part is xn_hi, stop=b == TB - 1 and part is xn_lo)
                    last.then_inc(gather_done, 1)

            def gathered_transposes():
                for h in range(2):
                    pe.wait_ge(rows_ready, seen.next(rows_ready))
                    for k in range(4):
                        last = nc.tensor.transpose(bank[6 + h][:, k * P:(k + 1) * P], tok_rows[:, (4 * h + k) * P:(4 * h + k + 1) * P],
                                                   ident[:, :])
                    last.then_inc(tokT_landed, 1)

            def spread_transposes():
                for b in range(TB):
                    last = nc.tensor.transpose(bank[3][:, b * P:(b + 1) * P], onehot[:, b, :].bitcast(F32), ident[:, :])
                last.then_inc(spreadT_landed, 1)

            def scatter(b, banks, after=False):
                for h in range(2):
                    if b == 0:
                        pe.wait_ge(y_ready, seen.next(y_ready))
                    elif after:
                        pe.wait_ge(scatter_added, seen.next(scatter_added))
                    part = slice(h * N, (h + 1) * N)
                    nc.tensor.matmul(bank[banks[h]][:, :], spreadT[:, b, :], y_hi[:, part], start=True, stop=False)
                    nc.tensor.matmul(bank[banks[h]][:, :], spreadT[:, b, :], y_lo[:, part], start=False,
                                     stop=True).then_inc(scatter_done, 1)

            gather()
            gathered_transposes()
            dense_silu = TB * (DC + 1)

            def item(i):
                for c in range(FC):
                    g = U0 + max(0, 6 * c - 2)
                    if c:
                        pe.wait_ge(silu_ready, seen.at(silu_ready, dense_silu + c))
                    slab(g, tokT_hi, tokT_lo, low[:1], fresh=tokT_ready if c == 0 else None,
                         between=(lambda: hidden_transposes(1, 4, 2)) if c else None)
                    slab(g + 2, tokT_hi, tokT_lo, low[1:])
                    if c == 1:
                        scatter(0, (6, 7))
                    if c == 2:
                        spread_transposes()
                    if c == 4:
                        pe.wait_ge(scatter_added, seen.next(scatter_added, 2))
                        pe.wait_ge(spreadT_ready, seen.next(spreadT_ready))
                        gather()
                    if c == 5:
                        gathered_transposes()
                    if c:
                        pe.wait_ge(actT_ready, seen.next(actT_ready))
                        rows(g + 4, 2, hidden(act_hi), hidden(act_lo), 1, 4, c == 1, False,
                             between=(lambda: hidden_transposes(1, 4, 2)) if c == FC - 1 else None)
                    if c == 1:
                        scatter(1, (6, 7), after=True)
                pe.wait_ge(actT_ready, seen.next(actT_ready))
                rows(U0 + UI - 2, 2, lambda f, b: act_hi[:, 1, f, :], lambda f, b: act_lo[:, 1, f, :], 1, 4, False, True)

            run_items(pe, seen, [0], item)
            scatter(0, (6, 7))
            scatter(1, (0, 1))


_INS = ["x", "mix_norm", "w_in", "conv_dw", "conv_dw_b", "conv_ln_g", "conv_ln_b", "w_conv_out", "w_pool", "pool_scale",
        "w_out", "ffn_norm", "dense_w_gate", "dense_w_up", "dense_w_down", "router_w", "moe_w_gate", "moe_w_up",
        "moe_w_down", "final_norm"]
_OUTS = [((1, 256, 1024), "float32")]


def kernel(**inputs):
    import numpy as _np
    import concourse.bacc as _bacc
    from concourse import mybir as _mybir
    from concourse.bass_utils import run_bass_kernel_spmd as _run

    nc = _bacc.Bacc("TRN2", target_bir_lowering=False, num_devices=1)
    arrays, args = {}, []
    for name in _INS:
        a = _np.ascontiguousarray(inputs[name])
        arrays[f"in_{name}_dram"] = a
        args.append(nc.dram_tensor(f"in_{name}_dram", a.shape, _mybir.dt.from_np(a.dtype), kind="ExternalInput").ap())
    for i, (shape, dtype) in enumerate(_OUTS):
        dt = _mybir.dt.from_np(_np.dtype(dtype))
        args.append(nc.dram_tensor(f"out_{i}_dram", shape, dt, kind="ExternalOutput").ap())
    trunk_kernel(nc, *args)
    r = _run(nc, [arrays], core_ids=[0])
    return r.results[0]["out_0_dram"]
```
